# Optimizing a Trainium2 kernel written in Bass

```python
import jax
import jax.numpy as jnp
from jax import lax
import numpy as np

D_MODEL = 2048
BATCH = 1
SEQ = 512
DEPTH = 1

HG_WIDTH = 1024
HG_HEADS = 8
HG_HEAD_DIM = HG_WIDTH // HG_HEADS
HG_CHUNK = 32
RW_WIDTH = 1024
RW_HEAD_DIM = 64
RW_HEADS = RW_WIDTH // RW_HEAD_DIM
RW_DECAY_LORA = 64
RW_AAA_LORA = 64
RW_MV_LORA = 32
RW_GATE_LORA = 160
RW_SHIFT_WIDTH = 3 * RW_WIDTH + RW_DECAY_LORA + RW_AAA_LORA + RW_GATE_LORA
IN_WIDTH = 4 * HG_WIDTH + RW_SHIFT_WIDTH + 2 * D_MODEL
IN_SPLITS = (HG_WIDTH, 2 * HG_WIDTH, 3 * HG_WIDTH, 4 * HG_WIDTH,
             4 * HG_WIDTH + RW_SHIFT_WIDTH, 4 * HG_WIDTH + RW_SHIFT_WIDTH + D_MODEL)
RW_SPLITS = (RW_WIDTH, 2 * RW_WIDTH, 3 * RW_WIDTH, 3 * RW_WIDTH + RW_DECAY_LORA,
             3 * RW_WIDTH + RW_DECAY_LORA + RW_AAA_LORA)
N_GROUPS = 4
EXPERTS_PER_GROUP = 8
N_EXPERTS = N_GROUPS * EXPERTS_PER_GROUP
TOP_K_IN_GROUP = 2
D_EXPERT = 512
DISPATCH_BLOCK = 128

NORM_EPS = 1e-6
RW_GN_EPS = 64e-5

kernel_name = 'hybrid_hgrn2_rwkv7_hier_moe'

def rmsnorm(x, w):
    xf = x.astype(jnp.float32)
    y = xf * lax.rsqrt(jnp.mean(xf * xf, axis=-1, keepdims=True) + NORM_EPS)
    return (y * w.astype(jnp.float32)).astype(x.dtype)

def token_shift(z):
    return jnp.pad(z, ((0, 0), (1, 0), (0, 0)))[:, :-1]

def hgrn2_chunked(q, k, v, log_f):
    bsz, seqlen, nh, dk = q.shape
    dv = v.shape[-1]
    n_chunks = seqlen // HG_CHUNK

    def to_chunks(t):
        return t.reshape(bsz, n_chunks, HG_CHUNK, nh, t.shape[-1]).transpose(1, 0, 3, 2, 4)

    causal = jnp.tril(jnp.ones((HG_CHUNK, HG_CHUNK), dtype=bool))[:, :, None]

    def step(state, inp):
        qc, kc, vc, gc = inp
        b = jnp.cumsum(gc, axis=2)
        o_inter = jnp.einsum('bhtd,bhde->bhte', qc * jnp.exp(b), state)
        diff = b[:, :, :, None, :] - b[:, :, None, :, :]
        decay = jnp.exp(jnp.where(causal, diff, -jnp.inf))
        scores = jnp.einsum('bhtd,bhsd,bhtsd->bhts', qc, kc, decay)
        o_intra = jnp.einsum('bhts,bhse->bhte', scores, vc)
        b_last = b[:, :, -1, :]
        k_dec = kc * jnp.exp(b_last[:, :, None, :] - b)
        state = jnp.exp(b_last)[..., None] * state + jnp.einsum('bhsd,bhse->bhde', k_dec, vc)
        return state, o_inter + o_intra

    s0 = jnp.zeros((bsz, nh, dk, dv), jnp.float32)
    _, o = lax.scan(step, s0, (to_chunks(q), to_chunks(k), to_chunks(v), to_chunks(log_f)))
    return o.transpose(1, 0, 3, 2, 4).reshape(bsz, seqlen, nh, dv)

def hgrn2_branch(zq, zf, zi, zo, lb, onorm_w):
    bsz, seqlen, _ = zq.shape
    heads = lambda t: t.reshape(bsz, seqlen, HG_HEADS, HG_HEAD_DIM)
    q = jax.nn.silu(zq.astype(jnp.float32))
    f_gate = lb + (1.0 - lb) * jax.nn.sigmoid(zf.astype(jnp.float32))
    o = hgrn2_chunked(heads(q), heads(1.0 - f_gate), heads(zi.astype(jnp.float32)),
                      heads(jnp.log(f_gate)))
    o = rmsnorm(o, onorm_w).reshape(bsz, seqlen, HG_WIDTH)
    return (o * jax.nn.sigmoid(zo.astype(jnp.float32))).astype(zq.dtype)

def rwkv7_scan(r, log_w, k, v, a_vec, b_vec):
    bsz, seqlen, nh, hd = r.shape
    tm = lambda t: t.transpose(1, 0, 2, 3)

    def step(state, inp):
        rt, lwt, kt, vt, at, bt = inp
        sa = jnp.einsum('bhvk,bhk->bhv', state, at)
        state = (state * jnp.exp(lwt)[:, :, None, :] + sa[..., None] * bt[:, :, None, :]
                 + vt[..., None] * kt[:, :, None, :])
        return state, jnp.einsum('bhvk,bhk->bhv', state, rt)

    s0 = jnp.zeros((bsz, nh, hd, hd), jnp.float32)
    _, y = lax.scan(step, s0, (tm(r), tm(log_w), tm(k), tm(v), tm(a_vec), tm(b_vec)))
    return y.transpose(1, 0, 2, 3)

def rwkv7_branch(zs, mu, w0, w_up, a0, a_up, g_up, k_k, k_a, r_k, ln_w, ln_b, v_first, v_res):
    bsz, seqlen, _ = zs.shape
    f32 = jnp.float32
    heads = lambda t: t.reshape(bsz, seqlen, RW_HEADS, RW_HEAD_DIM)
    zs = zs + mu * (token_shift(zs) - zs)
    r, k, v, wd, ad, gd = jnp.split(zs, RW_SPLITS, axis=-1)
    log_w = -jnp.exp(-jax.nn.softplus(-(w0 + jnp.tanh(wd) @ w_up).astype(f32)) - 0.5)
    a = jax.nn.sigmoid((a0 + ad @ a_up).astype(f32))
    g = jax.nn.sigmoid(gd) @ g_up
    if v_res is None:
        v_first = v
    else:
        v0, v_down, v_up = v_res
        v = v + (v_first - v) * jax.nn.sigmoid(v0 + (v @ v_down) @ v_up)
    kk = heads((k * k_k).astype(f32))
    kk = kk * lax.rsqrt(jnp.maximum(jnp.sum(kk * kk, axis=-1, keepdims=True), 1e-12))
    a_h = heads(a)
    k_h = heads(k.astype(f32) * (1.0 + (a - 1.0) * k_a.astype(f32)))
    r_h = heads(r.astype(f32))
    v_h = heads(v.astype(f32))
    y = rwkv7_scan(r_h, heads(log_w), k_h, v_h, -kk, kk * a_h)
    mean = jnp.mean(y, axis=-1, keepdims=True)
    var = jnp.mean(jnp.square(y - mean), axis=-1, keepdims=True)
    y = ((y - mean) * lax.rsqrt(var + RW_GN_EPS) * ln_w.astype(f32).reshape(RW_HEADS, RW_HEAD_DIM)
         + ln_b.astype(f32).reshape(RW_HEADS, RW_HEAD_DIM))
    y = y + jnp.sum(r_h * k_h * r_k.astype(f32), axis=-1, keepdims=True) * v_h
    y = y.reshape(bsz, seqlen, RW_WIDTH) * g.astype(f32)
    return y.astype(zs.dtype), v_first

def hier_moe(h, wg_r, bg_r, we_r, be_r, w_gate, w_up, w_down):
    bsz, seqlen, d = h.shape
    n_tok = bsz * seqlen
    hf = h.reshape(n_tok, d)
    f32 = jnp.float32
    g_logits = (hf @ wg_r + bg_r).astype(f32)
    g_prob = jax.nn.softmax(g_logits, axis=-1)
    g_sel = jnp.argmax(g_logits, axis=-1)
    p_group = jnp.take_along_axis(g_prob, g_sel[:, None], axis=-1)
    e_logits = (hf @ we_r + be_r).astype(f32).reshape(n_tok, N_GROUPS, EXPERTS_PER_GROUP)
    e_logits = jnp.take_along_axis(e_logits, g_sel[:, None, None], axis=1)[:, 0]
    top_l, top_i = lax.top_k(e_logits, TOP_K_IN_GROUP)
    weights = p_group * jax.nn.softmax(top_l, axis=-1)
    expert_id = g_sel[:, None] * EXPERTS_PER_GROUP + top_i
    n_assign = n_tok * TOP_K_IN_GROUP
    eid = expert_id.reshape(n_assign).astype(jnp.int32)
    w_flat = weights.reshape(n_assign)
    tok = jnp.repeat(jnp.arange(n_tok, dtype=jnp.int32), TOP_K_IN_GROUP)
    counts = jnp.bincount(eid, length=N_EXPERTS)
    padded = ((counts + DISPATCH_BLOCK - 1) // DISPATCH_BLOCK) * DISPATCH_BLOCK
    pad_end = jnp.cumsum(padded)
    pad_start = pad_end - padded
    start = jnp.cumsum(counts) - counts
    order = jnp.argsort(eid)
    se = eid[order]
    dest = pad_start[se] + (jnp.arange(n_assign, dtype=jnp.int32) - start[se])
    n_slots = n_assign + N_EXPERTS * DISPATCH_BLOCK
    n_blocks = n_slots // DISPATCH_BLOCK
    buf_tok = jnp.full((n_slots,), n_tok, jnp.int32).at[dest].set(tok[order])
    buf_w = jnp.zeros((n_slots,), f32).at[dest].set(w_flat[order])
    blk_e = jnp.clip(jnp.searchsorted(pad_end, jnp.arange(n_blocks) * DISPATCH_BLOCK, side='right'),
                     0, N_EXPERTS - 1)
    hpad = jnp.concatenate([hf, jnp.zeros((1, d), hf.dtype)], axis=0)
    xs = hpad[buf_tok].reshape(n_blocks, DISPATCH_BLOCK, d)

    def expert_block(args):
        xb, e = args
        return (jax.nn.silu(xb @ w_gate[e]) * (xb @ w_up[e])) @ w_down[e]

    ys = lax.map(expert_block, (xs, blk_e)).reshape(n_slots, d)
    out = jax.ops.segment_sum(ys * buf_w[:, None], buf_tok, num_segments=n_tok + 1)[:n_tok]
    return out.astype(h.dtype).reshape(bsz, seqlen, d)

def setup_inputs(seed: int = 0) -> dict:
    key = jax.random.key(seed)
    ks = jax.random.split(key, 40)
    counter = [0]

    def nxt():
        counter[0] += 1
        return ks[counter[0] - 1]

    def normal(shape, scale):
        return scale * jax.random.normal(nxt(), shape, jnp.float32)

    def gain(shape):
        return 1.0 + normal(shape, 0.02)

    L = DEPTH
    D = D_MODEL
    return {
        'x': normal((BATCH, SEQ, D), 1.0),
        'norm_mix_w': gain((L, D)),
        'w_in': normal((L, D, IN_WIDTH), D ** -0.5),
        'hgrn_lb_raw': normal((L, HG_WIDTH), 0.5),
        'hgrn_onorm_w': gain((L, HG_HEAD_DIM)),
        'rw_mu': jax.random.uniform(nxt(), (L, RW_SHIFT_WIDTH), jnp.float32),
        'rw_w0': jax.random.uniform(nxt(), (L, RW_WIDTH), jnp.float32, -3.0, 1.0),
        'rw_w_up': normal((L, RW_DECAY_LORA, RW_WIDTH), 0.1),
        'rw_a0': normal((L, RW_WIDTH), 0.1),
        'rw_a_up': normal((L, RW_AAA_LORA, RW_WIDTH), 0.1),
        'rw_g_up': normal((L, RW_GATE_LORA, RW_WIDTH), RW_GATE_LORA ** -0.5),
        'rw_k_k': 0.85 + normal((L, RW_WIDTH), 0.05),
        'rw_k_a': 1.0 + normal((L, RW_WIDTH), 0.05),
        'rw_r_k': normal((L, RW_HEADS, RW_HEAD_DIM), 0.1),
        'rw_ln_w': gain((L, RW_WIDTH)),
        'rw_ln_b': normal((L, RW_WIDTH), 0.02),
        'rw_v0': normal((L - 1, RW_WIDTH), 0.1),
        'rw_v_down': normal((L - 1, RW_WIDTH, RW_MV_LORA), RW_WIDTH ** -0.5),
        'rw_v_up': normal((L - 1, RW_MV_LORA, RW_WIDTH), 0.1),
        'w_branch_hg': normal((L, HG_WIDTH, D), HG_WIDTH ** -0.5),
        'w_branch_rw': normal((L, RW_WIDTH, D), RW_WIDTH ** -0.5),
        'w_out': normal((L, D, D), D ** -0.5),
        'norm_ffn_w': gain((L, D)),
        'router_group_w': normal((L, D, N_GROUPS), D ** -0.5),
        'router_group_b': normal((L, N_GROUPS), 0.01),
        'router_expert_w': normal((L, D, N_EXPERTS), D ** -0.5),
        'router_expert_b': normal((L, N_EXPERTS), 0.01),
        'expert_w_gate': normal((L, N_EXPERTS, D, D_EXPERT), D ** -0.5),
        'expert_w_up': normal((L, N_EXPERTS, D, D_EXPERT), D ** -0.5),
        'expert_w_down': normal((L, N_EXPERTS, D_EXPERT, D), D_EXPERT ** -0.5),
        'final_norm_w': gain((D,)),
    }

def reference(x, norm_mix_w, w_in, hgrn_lb_raw, hgrn_onorm_w, rw_mu, rw_w0, rw_w_up, rw_a0,
              rw_a_up, rw_g_up, rw_k_k, rw_k_a, rw_r_k, rw_ln_w, rw_ln_b, rw_v0, rw_v_down,
              rw_v_up, w_branch_hg, w_branch_rw, w_out, norm_ffn_w, router_group_w,
              router_group_b, router_expert_w, router_expert_b, expert_w_gate, expert_w_up,
              expert_w_down, final_norm_w):
    lb_all = jnp.cumsum(jax.nn.softmax(hgrn_lb_raw.astype(jnp.float32), axis=0), axis=0)
    lb_all = lb_all - lb_all[:1]
    h = x
    v_first = None
    for l in range(DEPTH):
        xn = rmsnorm(h, norm_mix_w[l])
        z = xn @ w_in[l]
        zq, zf, zi, zo, zs, zga, zgb = jnp.split(z, IN_SPLITS, axis=-1)
        y_hg = hgrn2_branch(zq, zf, zi, zo, lb_all[l], hgrn_onorm_w[l])
        v_res = None if l == 0 else (rw_v0[l - 1], rw_v_down[l - 1], rw_v_up[l - 1])
        y_rw, v_first = rwkv7_branch(zs, rw_mu[l], rw_w0[l], rw_w_up[l], rw_a0[l], rw_a_up[l],
                                     rw_g_up[l], rw_k_k[l], rw_k_a[l], rw_r_k[l], rw_ln_w[l],
                                     rw_ln_b[l], v_first, v_res)
        merged = (jax.nn.sigmoid(zga) * (y_hg @ w_branch_hg[l])
                  + jax.nn.sigmoid(zgb) * (y_rw @ w_branch_rw[l]))
        h = h + merged @ w_out[l]
        hn = rmsnorm(h, norm_ffn_w[l])
        h = h + hier_moe(hn, router_group_w[l], router_group_b[l], router_expert_w[l],
                         router_expert_b[l], expert_w_gate[l], expert_w_up[l], expert_w_down[l])
    return rmsnorm(h, final_norm_w)


_drawn_inputs = setup_inputs


def setup_inputs(seed=0):
    import zlib

    import numpy as np

    out = dict(_drawn_inputs(seed))
    spreads = {}
    factors = {'hgrn_onorm_w': 17.974,
     'rw_k_k': 13.528,
     'rw_ln_w': 16.135,
     'rw_ln_b': 15.918,
     'router_group_b': 26.477,
     'router_expert_b': 16.82,
     'final_norm_w': 7.665,
     'norm_ffn_w': 3.724}
    for name, (base, spread) in spreads.items():
        noise = np.random.default_rng([zlib.crc32(name.encode()), seed]).standard_normal(out[name].shape)
        drawn = base * np.exp(spread * noise) if base else spread * noise
        out[name] = jnp.asarray(drawn.astype(out[name].dtype))
    for name, factor in factors.items():
        out[name] = (out[name] * factor).astype(out[name].dtype)
    return out
```

```python
from contextlib import ExitStack

import numpy as np

import concourse.bass as bass
from concourse import mybir

ALU = mybir.AluOpType
ACT = mybir.ActivationFunctionType
F32 = mybir.dt.float32
F32R = mybir.dt.float32r
BF16 = mybir.dt.bfloat16
I32 = mybir.dt.int32
U32 = mybir.dt.uint32
AX_X = mybir.AxisListType.X

P = 128
D = 2048
T = 512
KT = D // P
TT = T // P
WIDTH = 1024
HEADS = WIDTH // P
HG_CHUNK = 32
RW_CHUNK = 64
RW_COL = 4 * WIDTH
LORA_COL = RW_COL + 3 * WIDTH
GATE_COL = LORA_COL + 288
N_GROUPS, PER_GROUP = 4, 8
N_EXPERTS = N_GROUPS * PER_GROUP
D_EXPERT = 512
SLOTS = 64
MAX_BLOCKS = 2 * T // SLOTS + N_EXPERTS
HG_GATES = 2
MIN_BLOCKS = 2 * T // SLOTS
TABLE_BLOCKS = MAX_BLOCKS + 4
NORM_EPS = 1e-6
GN_EPS = 64e-5
PASSES = 3
MAT_BANK = (2, 3, 4, 5, 0, 1, 2, 3)

CONST = {n: i for i, n in enumerate(
    ["ident", "ones", "block64", "strict64", "causal64", "causal32", "prefix", "ramp", "step1", "step2", "step4", "step8",
     "step16", "step32"])}
ROWS = {}
for _n, _k in (("mu_r", 8), ("mu_k", 8), ("mu_v", 8), ("mu_wa", 1), ("mu_g1", 1), ("mu_g2", 1), ("w0", 8), ("a0", 8),
               ("k_k", 8), ("k_a", 8), ("r_k", 8), ("ln_w", 8), ("ln_b", 8), ("lb", 8), ("onorm", 1),
               ("norm_mix", 16), ("norm_ffn", 16)):
    ROWS[_n] = (sum(k for _, k in ROWS.values()), _k)
N_ROWS = sum(k for _, k in ROWS.values())
assert N_ROWS <= P


def square_constants():
    s, t = np.arange(P)[:, None], np.arange(P)[None, :]
    x = s ^ t
    c = {"ident": s == t, "ones": s >= 0, "block64": (x < 64), "strict64": (x < 64) & (s < t),
         "causal64": (x < 64) & (s <= t), "causal32": (x < 32) & (s <= t), "prefix": s < t,
         "ramp": np.where(t == P - 1, s, t)}
    c["ones"] = np.broadcast_to(c["ones"], (P, P))
    for m in (1, 2, 4, 8, 16, 32):
        c[f"step{m}"] = (x >= m) & (x < 2 * m) & (s < t)
    return np.ascontiguousarray(np.stack([c[n] for n in CONST], 1).astype(np.float32))


class Memory:

    def __init__(self, nc, ctx):
        self.nc, self.ctx, self.sems = nc, ctx, []
        ctx.callback(self.clear)

    def clear(self):
        if self.sems:
            self.nc.clear_and_free_semaphores(self.sems)
            self.nc.all_engine_barrier()

    def sb(self, name, shape, dt=F32):
        return self.ctx.enter_context(self.nc.sbuf_tensor(name, shape, dt))

    def shared(self, first, second):
        with ExitStack() as short:
            a = short.enter_context(self.nc.sbuf_tensor(*first))
        return a, self.ctx.enter_context(self.nc.sbuf_tensor(*second))

    def psum(self, name, shape, dt=F32):
        return self.ctx.enter_context(self.nc.psum_tensor(name, shape, dt))

    def sem(self, *names):
        s = [self.nc.alloc_semaphore(n) for n in names]
        self.sems += s
        return s[0] if len(s) == 1 else s


class Order:

    def __init__(self, eng, sem, base=0):
        self.eng, self.sem, self.base, self.n = eng, sem, base, 0

    def done(self, ins):
        self.n += 1
        ins.then_inc(self.sem, 1)

    def wait(self):
        self.eng.wait_ge(self.sem, self.base + self.n)


def wait_apart(eng, passed, sem, value):
    eng.wait_ge(sem, value)
    eng.sem_inc(passed, 1)


def product(pe, out, w_hi, w_lo, x_hi, x_lo, first, last):
    pe.matmul(out, w_hi, x_hi, start=first, stop=False, skip_group_check=True)
    pe.matmul(out, w_hi, x_lo, start=False, stop=False, skip_group_check=True)
    return pe.matmul(out, w_lo, x_hi, start=False, stop=last, skip_group_check=True)


def dense_pass(pe, out, ring, slot, x_hi, x_lo, n):
    k, which = n // PASSES, n % PASSES
    w = ring["lo"][slot] if which == 2 else ring["hi"][slot]
    x = x_lo if which == 1 else x_hi
    return pe.matmul(out, w[:, k, :], x[:, k, :], start=(n == 0), stop=(n == PASSES * KT - 1), skip_group_check=True)


def make_ring(mem, tag, inner=(KT, P), depth=2):
    return {
        "raw": [mem.sb(f"{tag}_raw{s}", [P, *inner]) for s in range(depth)],
        "hi": [mem.sb(f"{tag}_hi{s}", [P, *inner], F32R) for s in range(depth)],
        "lo": [mem.sb(f"{tag}_lo{s}", [P, *inner], F32R) for s in range(depth)],
        "raw_in": [mem.sem(f"{tag}_raw_in{s}") for s in range(depth)],
        "hi_done": mem.sem(f"{tag}_hi_done"), "lo_done": mem.sem(f"{tag}_lo_done"),
        "unit_done": mem.sem(f"{tag}_unit_done"), "passed": mem.sem(f"{tag}_loads_passed"),
        "depth": depth,
    }


def ring_load(sp, ring, slot, m, src):
    wait_apart(sp, ring["passed"], ring["lo_done"], m + 1)
    sp.dma_start(ring["raw"][slot][:], src).then_inc(ring["raw_in"][slot], 16)


def ring_hi(act, ring, slot, m, turn):
    act.wait_ge(ring["raw_in"][slot], 16 * turn + 16)
    act.wait_ge(ring["unit_done"], m + 1)
    act.activation(ring["hi"][slot][:], ring["raw"][slot][:], ACT.Copy).then_inc(ring["hi_done"], 1)


def ring_lo(dve, ring, slot, m):
    dve.wait_ge(ring["hi_done"], m + 1)
    dve.tensor_tensor(ring["lo"][slot][:], ring["raw"][slot][:], ring["hi"][slot][:].bitcast(F32),
                      ALU.subtract).then_inc(ring["lo_done"], 1)


def ring_ready(pe, ring, m):
    pe.wait_ge(ring["lo_done"], m + 1 + ring["depth"])


def ring_used(eng, ring, m):
    eng.wait_ge(ring["unit_done"], m + 1 + ring["depth"])


def k_tiles(matrix):
    return matrix.rearrange("(k p) n -> p k n", p=P)


def phase_norm(nc, io, keep):
    with ExitStack() as ctx:
        mem = Memory(nc, ctx)
        x_sb = mem.sb("x_sb", [P, TT, D])
        sq = mem.sb("x_square", [P, D])
        rows = mem.sb("param_rows", [P, P])
        var, rstd, tmp = mem.sb("x_var", [P, TT]), mem.sb("x_rstd", [P, TT]), mem.sb("x_rstd_tmp", [P, TT])
        tr = [mem.psum(f"x_tr{b}", [P, T]) for b in range(4)]
        par_ps = mem.psum("param_ps", [P, P])
        x_in = [mem.sem(f"x_in{t}") for t in range(TT)]
        rows_in, const_in, zeroed = mem.sem("rows_in", "const_in", "rows_zeroed")
        sq_done, act_o, dve_o = mem.sem("sq_done", "norm_act_o", "norm_dve_o")
        scaled, turned, hi_done, lo_done = mem.sem("x_scaled", "x_turned", "xn_hi_done", "xn_lo_done")
        par_done, par_turned = mem.sem("par_done", "par_turned")
        block = ctx.enter_context(nc.Block())

        @block.sync
        def _(sp):
            for t in range(TT):
                sp.dma_start(x_sb[:, t, :], io["x"][0, t * P:(t + 1) * P, :]).then_inc(x_in[t], 16)
            sp.dma_start(keep["const"][:], io["square_constants"]).then_inc(const_in, 16)
            sp.wait_ge(zeroed, 1)
            mu = io["rw_mu"][0]
            lists = [(ROWS["mu_r"][0], mu[0:24 * P].rearrange("(a b) -> a b", b=P), 24),
                     (ROWS["mu_wa"][0], mu[24 * P:26 * P].rearrange("(a b) -> a b", b=P), 2),
                     (ROWS["mu_g2"][0], mu[26 * P - 96:26 * P + 32].rearrange("(a b) -> a b", b=P), 1)]
            for name, key in (("w0", "rw_w0"), ("a0", "rw_a0"), ("k_k", "rw_k_k"), ("k_a", "rw_k_a"),
                              ("ln_w", "rw_ln_w"), ("ln_b", "rw_ln_b"), ("lb", "hgrn_lb_raw"),
                              ("onorm", "hgrn_onorm_w"), ("norm_mix", "norm_mix_w"), ("norm_ffn", "norm_ffn_w")):
                lists.append((ROWS[name][0], io[key][0].rearrange("(a b) -> a b", b=P), ROWS[name][1]))
            lists.append((ROWS["r_k"][0], io["rw_r_k"][0].rearrange("(a c) d -> a (c d)", c=2), 8))
            for first, src, n in lists:
                sp.dma_start(rows[first:first + n, :], src).then_inc(rows_in, 16)

        @block.scalar
        def _(act):
            order = Order(act, act_o)
            for t in range(TT):
                act.wait_ge(x_in[t], 16)
                if t:
                    order.wait()
                order.done(act.activation(sq[:], x_sb[:, t, :], ACT.Square, accum_out=var[:, t:t + 1]))
            order.wait()
            act.wait_ge(dve_o, 1)
            act.activation(tmp[:], rstd[:], ACT.Sqrt).then_inc(sq_done, 1)
            act.wait_ge(par_done, 1)
            for k in range(KT):
                act.wait_ge(turned, k + 1)
                w = keep["par"][:, ROWS["norm_mix"][0] + k:ROWS["norm_mix"][0] + k + 1]
                act.activation(keep["xn_hi"][:, k, :], tr[k % 4][:], ACT.Copy, scale=w).then_inc(hi_done, 1)

        @block.vector
        def _(dve):
            order = Order(dve, dve_o)
            dve.memset(rows[:], 0.0).then_inc(zeroed, 1)
            dve.wait_ge(act_o, TT)
            order.done(dve.tensor_scalar(rstd[:], var[:], 1.0 / D, NORM_EPS, ALU.mult, ALU.add))
            dve.wait_ge(sq_done, 1)
            order.done(dve.reciprocal(var[:], tmp[:]))
            order.wait()
            order.done(dve.tensor_tensor(tmp[:], var[:], var[:], ALU.mult))
            order.wait()
            order.done(dve.tensor_tensor(tmp[:], tmp[:], rstd[:], ALU.mult))
            order.wait()
            order.done(dve.tensor_scalar(tmp[:], tmp[:], -0.5, 1.5, ALU.mult, ALU.add))
            order.wait()
            order.done(dve.tensor_tensor(rstd[:], tmp[:], var[:], ALU.mult))
            order.wait()
            for t in range(TT):
                dve.tensor_scalar(x_sb[:, t, :], x_sb[:, t, :], rstd[:, t:t + 1], None, ALU.mult).then_inc(scaled, 1)
            dve.wait_ge(par_turned, 1)
            dve.tensor_copy(keep["par"][:], par_ps[:]).then_inc(par_done, 1)
            dve.wait_ge(par_done, 1)
            dve.tensor_scalar(keep["one_ka"][:], keep["par"][:, ROWS["k_a"][0]:ROWS["k_a"][0] + 8], -1.0, 1.0,
                              ALU.mult, ALU.add)
            e, one, lb, rest = (keep["lb"][:, j, :] for j in range(4))
            raw = keep["par"][:, ROWS["lb"][0]:ROWS["lb"][0] + HEADS]
            order.done(dve.tensor_tensor(e, raw, raw, ALU.subtract))
            order.wait()
            order.done(dve.tensor_scalar(e, e, 1.0, None, ALU.add))
            order.wait()
            order.done(dve.reciprocal(one, e))
            order.wait()
            order.done(dve.tensor_tensor(one, one, e, ALU.mult))
            order.wait()
            order.done(dve.tensor_tensor(lb, one, one, ALU.subtract))
            order.wait()
            order.done(dve.tensor_scalar(rest, lb, -1.0, 1.0, ALU.mult, ALU.add))
            for k in range(KT):
                dve.wait_ge(hi_done, k + 1)
                w = keep["par"][:, ROWS["norm_mix"][0] + k:ROWS["norm_mix"][0] + k + 1]
                dve.scalar_tensor_tensor(keep["xn_lo"][:, k, :], tr[k % 4][:], w, keep["xn_hi"][:, k, :].bitcast(F32),
                                         ALU.mult, ALU.subtract).then_inc(lo_done, 1)

        @block.tensor
        def _(pe):
            ident = keep["const"][:, CONST["ident"], :]
            pe.wait_ge(const_in, 16)
            pe.wait_ge(rows_in, 16 * 14)
            pe.transpose(par_ps[:], rows[:], ident).then_inc(par_turned, 1)
            pe.wait_ge(scaled, TT)
            for k in range(KT):
                if k >= 4:
                    pe.wait_ge(lo_done, k - 3)
                for t in range(TT):
                    mm = pe.transpose(tr[k % 4][:, t * P:(t + 1) * P], x_sb[:, t, k * P:(k + 1) * P], ident)
                mm.then_inc(turned, 1)


def phase_hgrn(nc, io, keep):
    UNITS = 4 + HG_GATES
    N_CHUNKS = T // HG_CHUNK
    MID = HG_CHUNK // 2 - 1
    ACT_STEPS = 1
    w_in = k_tiles(io["w_in"][0])
    with ExitStack() as ctx:
        mem = Memory(nc, ctx)
        ring = make_ring(mem, "hg")
        z = [mem.psum(f"hg_z{b}", [P, T]) for b in range(2)]
        tr = [mem.psum(f"hg_tr{b}", [P, T]) for b in range(2)]
        sc, o_ps, u_ps, mn_ps = (mem.psum(n, [P, T]) for n in ("hg_sc", "hg_o", "hg_u", "hg_mn"))
        tmp_f, tmp_q, f_sb, k_sb, logf, cum, dm, dl, q_sb = (
            mem.sb("hg_" + n, [P, T]) for n in ("tmp_f", "tmp_q", "f", "k", "logf", "cum", "dm", "dl", "q"))
        e_mid, e_neg, e_cum, e_last = (mem.sb("hg_" + n, [P, T]) for n in ("e_mid", "e_neg", "e_cum", "e_last"))
        q_mid, q_cum, k_mid, k_last, v_t, o_gate = (
            mem.sb("hg_" + n, [P, T]) for n in ("q_mid", "q_cum", "k_mid", "k_last", "v_t", "o_gate"))
        g_last = mem.sb("hg_g_last", [P, N_CHUNKS])
        v_tok, k_tok, scores = (mem.sb("hg_" + n, [P, TT, P]) for n in ("v_tok", "k_tok", "scores"))
        state = [mem.sb(f"hg_state{s}", [P, P]) for s in range(2)]
        o_sq, rs = mem.sb("hg_o_sq", [P, T]), mem.sb("hg_rs", [P, T])
        y = mem.sb("hg_y", [P, T])
        gate = [mem.sb(f"gate{s}", [P, T]) for s in range(2)]
        reset = mem.sb("hg_reset", [P, T], BF16)
        eps = mem.sb("hg_eps", [P, 1])
        z_read = mem.sem("hg_z_read0", "hg_z_read1")
        dve_o, act_o, const_ready = mem.sem("hg_dve_o", "hg_act_o", "hg_const_ready")
        f_ready, logf_ready, decays_ready, exps_ready = mem.sem("f_ready", "logf_ready", "decays_ready", "exps_ready")
        q_sigmoid, qk_ready, turned, v_tok_ready, k_tok_ready = mem.sem(
            "q_sigmoid", "qk_ready", "hg_turned", "v_tok_ready", "k_tok_ready")
        scores_done, scores_ready, update_done, state_ready = mem.sem(
            "scores_done", "scores_ready", "update_done", "state_ready")
        o_done, sq_ready, mean_done, rs_ready, y_ready, y_stored = mem.sem(
            "o_done", "hg_sq_ready", "hg_mean_done", "hg_rs_ready", "hg_y_ready", "hg_y_stored")
        ys_cleared = mem.sem("ys_cleared")
        zeros = mem.sb("hg_zeros", [P, D])
        gate_stored, gate_free, y_free = mem.sem("gate_stored", "gate_free", "hg_y_free")
        chunked = lambda a: a[:].rearrange("p (c t) -> p c t", t=HG_CHUNK)
        block = ctx.enter_context(nc.Block())

        def columns(i, u):
            if u < 4:
                return (WIDTH, 0, 2 * WIDTH, 3 * WIDTH)[u] + P * i
            return GATE_COL + P * (u - 4) + HG_GATES * P * i

        @block.sync
        def _(sp):
            with sp.Fori(0, HEADS) as i:
                for u in range(UNITS):
                    ring_load(sp, ring, u % 2, UNITS * i + u, w_in[:, :, bass.ds(columns(i, u), P)])
            ring_load(sp, ring, 0, UNITS * HEADS, w_in[:, :, 0:P])

        @block.gpsimd
        def _(pool):
            pool.memset(eps[:], NORM_EPS)
            pool.memset(reset[:], 1.0).then_inc(const_ready, 1)
            pool.wait_ge(const_ready, 1)
            pool.memset(chunked(reset)[:, :, 0:1], 0.0).then_inc(const_ready, 1)
            pool.memset(zeros[:], 0.0).then_inc(const_ready, 1)
            pool.sem_inc(gate_free, 2)
            pool.sem_inc(y_free, 1)
            pool.wait_ge(const_ready, 3)

            def clear_ys(n):
                pool.dma_start(io["ys"][bass.ds(SLOTS * MIN_BLOCKS + P * n, P), :], zeros[:]).then_inc(ys_cleared, 16)

            assert (MAX_BLOCKS + 2 - MIN_BLOCKS) * SLOTS == (2 * HEADS + 1) * P
            clear_ys(2 * HEADS)
            with pool.Fori(0, HEADS) as i:
                for n in range(2):
                    clear_ys(2 * i + n)
                for g in range(HG_GATES):
                    wait_apart(pool, keep["pool_waits"], z_read[g % 2], UNITS // 2 * i + 2 + g // 2 + 2)
                    pool.dma_start(io["gate"][bass.ds(HG_GATES * i + g, 1)].rearrange("a p t -> p (a t)"),
                                   gate[g][:]).then_inc(gate_stored, 16)
                    pool.wait_ge(gate_stored, 16 * HG_GATES * i + 16 * g + 16)
                    pool.sem_inc(gate_free, 1)
                wait_apart(pool, keep["pool_waits"], y_ready, i + 1)
                pool.dma_start(io["y_hg"][bass.ds(i, 1)].rearrange("a p t -> p (a t)"), y[:]).then_inc(y_stored, 16)
                pool.wait_ge(y_stored, 16 * i + 16)
                pool.sem_inc(y_free, 1)
            pool.wait_ge(ys_cleared, 16 * (2 * HEADS + 1))

        @block.scalar
        def _(act):
            act.sem_inc(z_read[0], 1)
            ring_hi(act, ring, 0, 0, 0)
            act.wait_ge(const_ready, 2)
            with act.Fori(0, HEADS) as i:
                order = Order(act, act_o, ACT_STEPS * i)
                m = UNITS * i

                def sigmoid(u, out):
                    ring_used(act, ring, m + u)
                    return act.activation(out, z[u % 2][:], ACT.Sigmoid)

                def split(u):
                    ring_hi(act, ring, u % 2, m + u, UNITS // 2 * i + u // 2)

                for u in range(UNITS):
                    if u != 2:
                        split(u + 1)
                    if u == 0:
                        sigmoid(u, tmp_f[:]).then_inc(z_read[0], 1)
                    elif u == 1:
                        sigmoid(u, tmp_q[:]).then_inc(q_sigmoid, 1)
                        act.wait_ge(f_ready, i + 1)
                        act.activation(logf[:], f_sb[:], ACT.Ln).then_inc(logf_ready, 1)
                        split(3)
                        act.wait_ge(decays_ready, i + 1)
                        act.activation(e_mid[:], dm[:], ACT.Exp)
                        act.activation(e_neg[:], dm[:], ACT.Exp, scale=-1.0)
                        act.activation(e_cum[:], cum[:], ACT.Exp)
                        act.activation(g_last[:], chunked(cum)[:, :, HG_CHUNK - 1], ACT.Exp)
                        act.activation(e_last[:], dl[:], ACT.Exp).then_inc(exps_ready, 1)
                    elif u == 2:
                        ring_used(act, ring, m + u)
                        act.activation(v_t[:], z[0][:], ACT.Copy).then_inc(z_read[0], 1)
                    elif u == 3:
                        act.wait_ge(turned, 2 * i + 1)
                        act.activation(v_tok[:], tr[0][:].rearrange("p (a b) -> p a b", b=P),
                                       ACT.Copy).then_inc(v_tok_ready, 1)
                        sigmoid(u, o_gate[:]).then_inc(z_read[1], 1)
                    else:
                        if u == UNITS - 1:
                            act.wait_ge(o_done, i + 1)
                            act.activation(o_sq[:], o_ps[:], ACT.Square).then_inc(sq_ready, 1)
                        act.wait_ge(gate_free, HG_GATES * i + u - 4 + 1)
                        sigmoid(u, gate[u % 2][:]).then_inc(z_read[u % 2], 1)
                act.wait_ge(mean_done, i + 1)
                order.done(act.activation(rs[:], mn_ps[:], ACT.Ln, bias=eps[:], scale=1.0 / P))
                order.wait()
                act.activation(rs[:], rs[:], ACT.Exp, scale=-0.5).then_inc(rs_ready, 1)
                assert order.n == ACT_STEPS, order.n

        @block.vector
        def _(dve):
            dve.sem_inc(ring["lo_done"], 2)
            dve.sem_inc(z_read[1], 1)
            ring_lo(dve, ring, 0, 0)
            dve.wait_ge(const_ready, 2)
            mask = keep["const"][:, CONST["causal32"], :].rearrange("p (a t) -> p a t", a=1).to_broadcast([P, TT, P])
            STEPS = 3
            with dve.Fori(0, HEADS) as i:
                order = Order(dve, dve_o, STEPS * i)
                m = UNITS * i

                def state_step(c):
                    dve.wait_ge(update_done, (N_CHUNKS - 1) * i + c + 1)
                    u = u_ps[:, P * (c % 2):P * (c % 2) + P]
                    if c == 0:
                        ins = dve.tensor_copy(state[1][:], u)
                    else:
                        dve.wait_ge(state_ready, (N_CHUNKS - 1) * i + c)
                        ins = dve.scalar_tensor_tensor(state[(c + 1) % 2][:], state[c % 2][:], g_last[:, c:c + 1], u,
                                                       ALU.mult, ALU.add)
                    ins.then_inc(state_ready, 1)

                ring_lo(dve, ring, 1, m + 1)
                dve.wait_ge(z_read[0], UNITS // 2 * i + 2)
                dve.tensor_scalar(f_sb[:], tmp_f[:], keep["lb"][:, 3, bass.ds(i, 1)], keep["lb"][:, 2, bass.ds(i, 1)],
                                  ALU.mult, ALU.add).then_inc(f_ready, 1)
                dve.wait_ge(f_ready, i + 1)
                order.done(dve.tensor_scalar(k_sb[:], f_sb[:], -1.0, 1.0, ALU.mult, ALU.add))
                ring_lo(dve, ring, 0, m + 2)
                dve.wait_ge(q_sigmoid, i + 1)
                dve.tensor_tensor(q_sb[:], z[1][:], tmp_q[:], ALU.mult).then_inc(z_read[1], 1)
                dve.wait_ge(logf_ready, i + 1)
                order.done(dve.tensor_tensor_scan(cum[:], reset[:], logf[:], 0.0, ALU.mult, ALU.add))
                order.wait()
                cum_c = chunked(cum)
                dve.tensor_tensor(chunked(dm), cum_c, cum_c[:, :, MID:MID + 1].to_broadcast([P, N_CHUNKS, HG_CHUNK]),
                                  ALU.subtract)
                dve.tensor_tensor(chunked(dl), cum_c[:, :, HG_CHUNK - 1:HG_CHUNK].to_broadcast([P, N_CHUNKS, HG_CHUNK]),
                                  cum_c, ALU.subtract).then_inc(decays_ready, 1)
                ring_lo(dve, ring, 1, m + 3)
                dve.wait_ge(z_read[1], UNITS // 2 * i + 2)
                dve.wait_ge(exps_ready, i + 1)
                dve.tensor_tensor(q_mid[:], q_sb[:], e_mid[:], ALU.mult)
                dve.tensor_tensor(q_cum[:], q_sb[:], e_cum[:], ALU.mult)
                dve.tensor_tensor(k_mid[:], k_sb[:], e_neg[:], ALU.mult)
                dve.tensor_tensor(k_last[:], k_sb[:], e_last[:], ALU.mult).then_inc(qk_ready, 1)
                dve.wait_ge(scores_done, i + 1)
                dve.tensor_tensor(scores[:], sc[:].rearrange("p (a b) -> p a b", b=P), mask,
                                  ALU.mult).then_inc(scores_ready, 1)
                dve.wait_ge(turned, 2 * i + 2)
                dve.tensor_copy(k_tok[:], tr[1][:].rearrange("p (a b) -> p a b", b=P)).then_inc(k_tok_ready, 1)
                splits = {1: 4, 6: 5, 13: 6}
                for c in range(N_CHUNKS - 1):
                    if c in splits:
                        ring_lo(dve, ring, splits[c] % 2, m + splits[c])
                    state_step(c)
                dve.wait_ge(rs_ready, i + 1)
                order.done(dve.tensor_tensor(o_sq[:], o_ps[:], rs[:], ALU.mult))
                order.wait()
                dve.wait_ge(y_free, i + 1)
                on = keep["par"][:, ROWS["onorm"][0]:ROWS["onorm"][0] + 1]
                dve.scalar_tensor_tensor(y[:], o_sq[:], on, o_gate[:], ALU.mult, ALU.mult).then_inc(y_ready, 1)
                assert order.n == STEPS, order.n

        @block.tensor
        def _(pe):
            pe.sem_inc(ring["unit_done"], 2)
            ident = keep["const"][:, CONST["ident"], :]
            with pe.Fori(0, HEADS) as i:
                m = UNITS * i

                def dense(u, n):
                    if n == 0:
                        ring_ready(pe, ring, m + u)
                        pe.wait_ge(z_read[u % 2], UNITS // 2 * i + u // 2 + 1)
                    mm = dense_pass(pe, z[u % 2][:], ring, u % 2, keep["xn_hi"], keep["xn_lo"], n)
                    if n == PASSES * KT - 1:
                        mm.then_inc(ring["unit_done"], 1)

                per_chunk = 3 * PASSES * KT // (N_CHUNKS + 4)
                for u in range(3):
                    for n in range(PASSES * KT):
                        dense(u, n)
                for n in range(2 * per_chunk):
                    dense(3, n)
                pe.wait_ge(z_read[0], UNITS // 2 * i + 3)
                for t in range(TT):
                    mm = pe.transpose(tr[0][:, t * P:(t + 1) * P], v_t[:, t * P:(t + 1) * P], ident)
                mm.then_inc(turned, 1)
                pe.wait_ge(qk_ready, i + 1)
                for t in range(TT):
                    mm = pe.transpose(tr[1][:, t * P:(t + 1) * P], k_last[:, t * P:(t + 1) * P], ident)
                mm.then_inc(turned, 1)
                for t in range(TT):
                    s = slice(t * P, (t + 1) * P)
                    mm = pe.matmul(sc[:, s], k_mid[:, s], q_mid[:, s], start=True, stop=True)
                mm.then_inc(scores_done, 1)
                for n in range(2 * per_chunk, 3 * per_chunk):
                    dense(3, n)
                pe.wait_ge(scores_ready, i + 1)
                pe.wait_ge(v_tok_ready, i + 1)
                pe.wait_ge(k_tok_ready, i + 1)
                for c in range(N_CHUNKS):
                    t, r = c // 4, HG_CHUNK * (c % 4)
                    if c % 4 == 0:
                        mm = pe.matmul(o_ps[:, t * P:(t + 1) * P], v_tok[:, t, :], scores[:, t, :], start=True, stop=False,
                                       skip_group_check=True)
                    if c:
                        pe.wait_ge(state_ready, (N_CHUNKS - 1) * i + c)
                        s = slice(c * HG_CHUNK, (c + 1) * HG_CHUNK)
                        mm = pe.matmul(o_ps[:, s], state[c % 2][:], q_cum[:, s], start=False, stop=(c % 4 == 3),
                                       skip_group_check=True)
                    if c < N_CHUNKS - 1:
                        pe.matmul(u_ps[:, P * (c % 2):P * (c % 2) + P], k_tok[r:r + HG_CHUNK, t, :],
                                  v_tok[r:r + HG_CHUNK, t, :], start=True, stop=True,
                                  skip_group_check=True).then_inc(update_done, 1)
                    if c == N_CHUNKS - 1:
                        mm.then_inc(o_done, 1)
                    for n in range((c + 3) * per_chunk, (c + 4) * per_chunk if c < N_CHUNKS - 1 else 3 * PASSES * KT):
                        dense(3 + n // (PASSES * KT), n % (PASSES * KT))
                pe.wait_ge(sq_ready, i + 1)
                pe.matmul(mn_ps[:], keep["const"][:, CONST["ones"], :], o_sq[:], start=True, stop=True).then_inc(mean_done, 1)



def phase_rwkv(nc, io, keep):
    PAIRS = HEADS
    N_CHUNKS = T // RW_CHUNK
    LEVELS = (2, 4, 8, 16, 32)
    HALF = P // 2
    FIRST = 3 + 3
    UNITS = 3 + HG_GATES
    DECAY = float(np.exp(-0.5))
    DVE_STEPS = 26
    ACT_STEPS = 2
    w_in = k_tiles(io["w_in"][0])
    with ExitStack() as ctx:
        mem = Memory(nc, ctx)
        ring = make_ring(mem, "rw")
        z = [mem.psum(f"rw_z{b}", [P, T]) for b in range(2)]
        bank = [mem.psum(f"rw_b{b}", [P, T]) for b in range(6)]
        zc = [mem.sb(f"rw_zc{u}", [P, T + 1]) for u in range(3)]
        r, k, v, g, akv_flat, e_a, kk, sq, cum, lw, cum_x, dl, e_cum, e_neg, kh, kt, ba, bonus = (
            mem.sb("rw_" + n, [P, T]) for n in (
                "r", "k", "v", "g", "akv", "e_a", "kk", "sq", "cum", "lw", "cum_x", "dl", "e_cum", "e_neg", "kh", "kt",
                "ba", "bonus"))
        v_tok, a_tok, b_tok, k_tok = (mem.sb("rw_" + n, [P, TT, P]) for n in ("v_tok", "a_tok", "b_tok", "k_tok"))
        ab, a_mat, xt, x_mat, ak, rb, rk = (mem.sb("rw_" + n, [P, 2, TT, P]) for n in (
            "ab", "a_mat", "xt", "x_mat", "ak", "rb", "rk"))
        t_mat = ab
        state = [mem.sb(f"rw_state{s}", [P, P]) for s in range(2)]
        g_last = mem.sb("rw_g_last", [P, N_CHUNKS])
        cols, one_ka, mus = mem.sb("rw_cols", [P, 7, 1]), mem.sb("rw_one_ka", [P, 1, 1]), mem.sb("rw_mus", [P, 3, 1])
        w_wa, w_g1, w_g2 = (mem.sb("rw_" + n, [P, P]) for n in ("w_wa", "w_g1", "w_g2"))
        low = [mem.sb(f"rw_low{u}", [P, T]) for u in range(3)]
        reset = mem.sb("rw_reset", [P, T], BF16)
        eps = mem.sb("rw_eps", [P, 1])
        akv, w_tok, u_tok = (b[:].rearrange("p (t f) -> p t f", f=P) for b in (akv_flat, e_a, sq))
        a_inv = kk
        y_sb, y_mid, y_out, g_rs = cum, lw, kt, ba
        rt, bt, at, bd, kd = e_cum, e_neg, cum_x, dl, kh
        gates = lambda last: (r[:], k[:]) if last else [x_mat[:, g].rearrange("p t f -> p (t f)") for g in range(HG_GATES)]
        W0, A0, K_K, K_A, R_K, LN_W, LN_B = range(7)
        sq4 = lambda a: a.rearrange("p (t f) -> p t f", f=P)
        chunked = lambda a: a[:].rearrange("p (c t) -> p c t", t=RW_CHUNK)
        z_read = mem.sem("rw_z_read0", "rw_z_read1")
        dve_o, act_o, const_ready, low_copied, low_ready = mem.sem("rw_dve_o", "rw_act_o", "rw_const_ready", "low_copied",
                                                                   "low_ready")
        lora_in, lora_done, mixed = mem.sem("lora_in", "lora_done", "rw_mixed")
        w_a_ready, g_ready, kk_ready, kk_sq, kk_sum, kk_max, kk_rs = mem.sem(
            "w_a_ready", "g_ready", "kk_ready", "kk_sq", "kk_sum", "kk_max", "kk_rs")
        decays_ready, exps_ready, operands_ready = mem.sem("rw_decays_ready", "rw_exps_ready", "operands_ready")
        tok_done, tok_by_act, tok_by_dve, mats_done, mats_ready = mem.sem(
            "tok_done", "tok_by_act", "tok_by_dve", "mats_done", "mats_ready")
        a_done, a_ready, xt_ready, xtr_done, x_ready, t_done, t_ready, xmul_done = mem.sem(
            "a_done", "a_ready", "xt_ready", "xtr_done", "x_ready", "t_done", "t_ready", "xmul_done")
        tail_done, tail_ready, u_done, u_ready, s_done, s_ready, s_zero = mem.sem(
            "tail_done", "tail_ready", "u_done", "u_ready", "s_done", "rw_s_ready", "s_zero")
        y_done, y_copied, mean_done, y_centered, y_sq, var_done, y_rs, bonus_sum = mem.sem(
            "rw_y_done", "y_copied", "rw_mean_done", "y_centered", "y_sq", "rw_var_done", "y_rs", "bonus_sum")
        y_ready, y_stored, y_free = mem.sem("rw_y_ready", "rw_y_stored", "rw_y_free")
        gate_stored, gate_free = mem.sem("rw_gate_stored", "rw_gate_free")
        block = ctx.enter_context(nc.Block())

        @block.sync
        def _(sp):
            for u in range(3):
                ring_load(sp, ring, u % 2, u, w_in[:, :, (LORA_COL, LORA_COL + P, LORA_COL + 288 - P)[u]:][:, :, 0:P])

            def lora(p, col):
                wait_apart(sp, ring["passed"], lora_done, 3 * p + 3)
                up = lambda w: w[:, bass.ds(col, P)]
                sp.dma_start(w_wa[0:HALF, :], up(io["rw_w_up"][0])).then_inc(lora_in, 16)
                sp.dma_start(w_wa[HALF:P, :], up(io["rw_a_up"][0])).then_inc(lora_in, 16)
                sp.dma_start(w_g1[:], up(io["rw_g_up"][0][0:P, :])).then_inc(lora_in, 16)
                sp.dma_start(w_g2[96:P, :], up(io["rw_g_up"][0][P:, :])).then_inc(lora_in, 16)

            def pair_units(p, q, last):
                cols = [] if last else [RW_COL + WIDTH * u + P * (p + 1) for u in range(3)]
                cols += [GATE_COL + P * (HG_GATES * (HEADS + p) + g) for g in range(HG_GATES)]
                for u, col in enumerate(cols):
                    ring_load(sp, ring, (q + u) % 2, FIRST + UNITS * p + u, w_in[:, :, bass.ds(col, P)])

            for u in range(3):
                ring_load(sp, ring, (3 + u) % 2, 3 + u, w_in[:, :, RW_COL + WIDTH * u:RW_COL + WIDTH * u + P])
            with sp.Fori(0, PAIRS // 2 - 1) as j:
                for q in range(2):
                    lora(2 * j + q, P * (2 * j + q))
                    pair_units(2 * j + q, q, False)
            for q in range(2):
                lora(PAIRS - 2 + q, P * (PAIRS - 2 + q))
                pair_units(PAIRS - 2 + q, q, q == 1)

        @block.gpsimd
        def _(pool):
            pool.memset(eps[:], GN_EPS)
            pool.memset(w_g2[0:96, :], 0.0)
            for s in range(2):
                pool.memset(state[s][:], 0.0)
            for u in range(3):
                pool.memset(zc[u][:, 0:1], 0.0)
            pool.memset(reset[:], 1.0).then_inc(const_ready, 1)
            pool.wait_ge(const_ready, 1)
            pool.memset(chunked(reset)[:, :, 0:1], 0.0).then_inc(const_ready, 1)
            pool.sem_inc(y_free, 1)
            pool.sem_inc(gate_free, 1)

            def store(p, q, half, last):
                def store_gate(g):
                    u = g if last else 3 + g
                    wait_apart(pool, keep["pool_waits"], z_read[(q + u) % 2], UNITS * half + (FIRST + UNITS * q + u) // 2 + 2)
                    pool.dma_start(io["gate"][bass.ds(HG_GATES * (HEADS + p) + g, 1)].rearrange("a p t -> p (a t)"),
                                   gates(last)[g]).then_inc(gate_stored, 16)

                store_gate(0)
                if last:
                    store_gate(1)
                wait_apart(pool, keep["pool_waits"], y_ready, p + 1)
                pool.dma_start(io["y_rw"][bass.ds(p, 1)].rearrange("a p t -> p (a t)"), y_out[:]).then_inc(y_stored, 16)
                if not last:
                    store_gate(1)
                pool.wait_ge(y_stored, 16 * p + 16)
                pool.sem_inc(y_free, 1)
                pool.wait_ge(gate_stored, 16 * HG_GATES * (p + 1))
                pool.sem_inc(gate_free, 1)

            with pool.Fori(0, PAIRS // 2 - 1) as j:
                for q in range(2):
                    store(2 * j + q, q, j, False)
            for q in range(2):
                store(PAIRS - 2 + q, q, PAIRS // 2 - 1, q == 1)

        @block.scalar
        def _(act):
            act.sem_inc(z_read[0], 1)
            act.sem_inc(z_read[1], 1)
            act.sem_inc(y_rs, 1)
            act.wait_ge(const_ready, 2)

            def copy_out(m, u, slot):
                ring_used(act, ring, m)
                act.activation(zc[u][:, 1:T + 1], z[slot][:], ACT.Copy).then_inc(z_read[slot], 1)

            ring_hi(act, ring, 0, 0, 0)
            ring_hi(act, ring, 1, 1, 0)
            copy_out(0, 0, 0)
            ring_hi(act, ring, 0, 2, 1)
            copy_out(1, 1, 1)
            ring_hi(act, ring, 1, 3, 1)
            copy_out(2, 2, 0)
            ring_hi(act, ring, 0, 4, 2)
            act.wait_ge(low_copied, 1)
            act.activation(low[0][0:HALF, :], low[0][0:HALF, :], ACT.Tanh).then_inc(low_ready, 1)
            act.wait_ge(low_copied, 3)
            for u in (1, 2):
                act.activation(low[u][:], low[u][:], ACT.Sigmoid).then_inc(low_ready, 1)
            copy_out(3, 0, 1)
            ring_hi(act, ring, 1, 5, 2)
            copy_out(4, 1, 0)
            ring_hi(act, ring, 0, 6, 3)
            copy_out(5, 2, 1)

            def pair(p, q, half, last):
                order = Order(act, act_o, ACT_STEPS * p)
                m = FIRST + UNITS * p
                count = HG_GATES if last else UNITS

                def split(u):
                    ring_hi(act, ring, (q + u) % 2, m + u, UNITS * half + (FIRST + UNITS * q + u) // 2)

                def read_out(u):
                    g = u - count + HG_GATES
                    if g < 0:
                        copy_out(m + u, u, (q + u) % 2)
                    else:
                        ring_used(act, ring, m + u)
                        act.activation(gates(last)[g], z[(q + u) % 2][:], ACT.Sigmoid).then_inc(z_read[(q + u) % 2], 1)

                split(1)
                act.wait_ge(lora_done, 3 * p + 4)
                act.wait_ge(mixed, p + 4)
                act.activation(lw[:], bank[0][:], ACT.Sigmoid, bias=cols[:, W0, :]).then_inc(w_a_ready, 1)
                act.wait_ge(kk_ready, p + 1)
                act.activation(sq[:], kk[:], ACT.Square).then_inc(kk_sq, 1)
                act.wait_ge(lora_done, 3 * p + 5)
                act.activation(e_a[:], bank[1][:], ACT.Sigmoid, bias=cols[:, A0, :]).then_inc(w_a_ready, 1)
                act.wait_ge(lora_done, 3 * p + 6)
                act.activation(g[:], bank[2][:], ACT.Copy).then_inc(g_ready, 1)
                act.wait_ge(kk_max, p + 1)
                order.done(act.activation(sq[:], sq[:], ACT.Ln))
                order.wait()
                act.activation(sq[:], sq[:], ACT.Exp, scale=-0.5).then_inc(kk_rs, 1)
                act.wait_ge(decays_ready, p + 1)
                act.activation(e_neg[:], cum[:], ACT.Exp, scale=DECAY)
                act.activation(e_cum[:], cum[:], ACT.Exp, scale=-DECAY)
                act.activation(g_last[:], chunked(cum)[:, :, RW_CHUNK - 1], ACT.Exp, scale=-DECAY)
                act.activation(cum_x[:], cum_x[:], ACT.Exp, scale=-DECAY)
                act.activation(dl[:], dl[:], ACT.Exp, scale=-DECAY).then_inc(exps_ready, 1)
                act.wait_ge(tok_done, 4 * p + 1)
                act.activation(v_tok[:], sq4(bank[4][:]), ACT.Copy).then_inc(tok_by_act, 1)
                act.wait_ge(tok_done, 4 * p + 2)
                act.activation(a_tok[:], sq4(bank[5][:]), ACT.Copy).then_inc(tok_by_act, 1)
                read_out(0)
                if not last:
                    split(2)
                act.wait_ge(gate_free, p + 1)
                for h in range(2):
                    act.wait_ge(a_done, 2 * p + h + 1)
                    act.activation(a_mat[:, h], sq4(bank[4 + h][:]), ACT.Copy).then_inc(a_ready, 1)
                for lv in range(len(LEVELS)):
                    for h in range(2):
                        act.wait_ge(xtr_done, 10 * p + 2 * lv + h + 1)
                        act.activation(x_mat[:, h], sq4(bank[4 + h][:]), ACT.Copy).then_inc(x_ready, 1)
                    if lv == 0:
                        read_out(1)
                    if not last and lv == 1:
                        split(3)
                    if not last and lv == 4:
                        read_out(2)
                        split(4)
                for n, dst in enumerate((akv, w_tok, a_inv[:].rearrange("p (t f) -> p t f", f=P))):
                    act.wait_ge(tail_done, 3 * p + n + 1)
                    act.activation(dst, sq4(bank[n][:]), ACT.Copy).then_inc(tail_ready, 1)
                if not last:
                    split(5)
                    read_out(3)
                act.wait_ge(y_done, p + 1)
                act.activation(y_sb[:], bank[5][:], ACT.Copy).then_inc(y_copied, 1)
                act.wait_ge(y_centered, p + 1)
                act.activation(sq[:], y_mid[:], ACT.Square).then_inc(y_sq, 1)
                act.wait_ge(var_done, p + 1)
                order.done(act.activation(g_rs[:], bank[1][:], ACT.Ln, bias=eps[:], scale=1.0 / HALF))
                order.wait()
                act.activation(g_rs[:], g_rs[:], ACT.Exp, scale=-0.5).then_inc(y_rs, 1)
                if not last:
                    read_out(4)
                assert order.n == ACT_STEPS

            with act.Fori(0, PAIRS // 2 - 1) as j:
                for q in range(2):
                    pair(2 * j + q, q, j, False)
            for q in range(2):
                pair(PAIRS - 2 + q, q, PAIRS // 2 - 1, q == 1)

        @block.vector
        def _(dve):
            const = lambda n: keep["const"][:, CONST[n], :].rearrange("p (a t) -> p a t", a=1).to_broadcast([P, TT, P])
            dve.sem_inc(ring["lo_done"], 2)
            dve.wait_ge(const_ready, 2)
            order0 = Order(dve, low_copied)
            mu = keep["par"][:, ROWS["mu_wa"][0]:ROWS["mu_wa"][0] + 3]

            def low_mix(u, slot, count):
                dve.wait_ge(z_read[slot], count)
                dve.tensor_tensor(y_sb[:], zc[u][:, 0:T], zc[u][:, 1:T + 1], ALU.subtract).then_inc(mixed, 1)
                dve.wait_ge(mixed, u + 1)
                order0.done(dve.scalar_tensor_tensor(low[u][:], y_sb[:], mu[:, u:u + 1], zc[u][:, 1:T + 1], ALU.mult, ALU.add))
                order0.wait()

            ring_lo(dve, ring, 0, 0)
            ring_lo(dve, ring, 1, 1)
            low_mix(0, 0, 2)
            ring_lo(dve, ring, 0, 2)
            low_mix(1, 1, 2)
            ring_lo(dve, ring, 1, 3)
            low_mix(2, 0, 3)
            ring_lo(dve, ring, 0, 4)
            ring_lo(dve, ring, 1, 5)
            ring_lo(dve, ring, 0, 6)

            def pair(p, q, half, last):
                order = Order(dve, dve_o, DVE_STEPS * p)
                tt = dve.tensor_tensor
                split = lambda u: ring_lo(dve, ring, (q + u) % 2, FIRST + UNITS * p + u)
                split(1)
                at_pair = lambda a, first, n: a[:, first:first + 8 * n].rearrange("p (a b) -> p a b", b=8)[:, :, bass.ds(p, 1)]
                order.done(dve.tensor_copy(mus[:], at_pair(keep["par"], 0, 3)))
                order.done(dve.tensor_copy(cols[:], at_pair(keep["par"], ROWS["w0"][0], 7)))
                order.done(dve.tensor_copy(one_ka[:], at_pair(keep["one_ka"], 0, 1)))
                order.wait()
                for u in (1, 2):
                    n = FIRST + UNITS * (q - 1) + u
                    dve.wait_ge(z_read[n % 2], UNITS * half + n // 2 + 2)
                for src, dst, tmp, n in ((zc[0], r, cum, 0), (zc[1], k, lw, 1), (zc[2], v, kt, 2)):
                    if n == 2:
                        dve.wait_ge(y_free, p + 1)
                    order.done(tt(tmp[:], src[:, 0:T], src[:, 1:T + 1], ALU.subtract))
                order.wait()
                for src, dst, tmp, n in ((zc[0], r, cum, 0), (zc[1], k, lw, 1), (zc[2], v, kt, 2)):
                    ins = dve.scalar_tensor_tensor(dst[:], tmp[:], mus[:, n, :], src[:, 1:T + 1], ALU.mult, ALU.add)
                    if n < 2:
                        order.done(ins)
                ins.then_inc(mixed, 1)
                order.wait()
                dve.tensor_scalar(kk[:], k[:], cols[:, K_K, :], None, ALU.mult).then_inc(kk_ready, 1)
                dve.wait_ge(w_a_ready, 2 * p + 1)
                order.done(dve.tensor_tensor_scan(cum[:], reset[:], lw[:], 0.0, ALU.mult, ALU.add))
                order.wait()
                order.done(tt(cum_x[:], cum[:], lw[:], ALU.subtract))
                cum_c = chunked(cum)
                tt(chunked(dl), cum_c[:, :, RW_CHUNK - 1:RW_CHUNK].to_broadcast([P, N_CHUNKS, RW_CHUNK]), cum_c,
                   ALU.subtract).then_inc(decays_ready, 1)
                dve.wait_ge(kk_sum, p + 1)
                dve.tensor_scalar(sq[:], bank[3][:], 1e-12, None, ALU.max).then_inc(kk_max, 1)
                dve.wait_ge(w_a_ready, 2 * p + 2)
                order.done(dve.tensor_scalar(kh[:], e_a[:], cols[:, K_A, :], one_ka[:, 0, :], ALU.mult, ALU.add))
                order.wait()
                order.done(tt(kh[:], kh[:], k[:], ALU.mult))
                order.wait()
                order.done(dve.scalar_tensor_tensor(bonus[:], r[:], cols[:, R_K, :], kh[:], ALU.mult, ALU.mult))
                dve.wait_ge(kk_rs, p + 1)
                order.done(tt(kk[:], kk[:], sq[:], ALU.mult))
                order.wait()
                order.done(tt(ba[:], kk[:], e_a[:], ALU.mult))
                order.wait()
                dve.wait_ge(exps_ready, p + 1)
                order.done(dve.scalar_tensor_tensor(at[:], kk[:], -1.0, cum_x[:], ALU.mult, ALU.mult))
                order.done(tt(kt[:], kh[:], e_neg[:], ALU.mult))
                order.done(tt(rt[:], r[:], e_cum[:], ALU.mult))
                order.wait()
                tt(bt[:], ba[:], e_neg[:], ALU.mult).then_inc(operands_ready, 1)
                order.done(tt(kd[:], kh[:], dl[:], ALU.mult))
                order.wait()
                tt(bd[:], ba[:], dl[:], ALU.mult).then_inc(operands_ready, 1)
                for n, dst in enumerate((b_tok, k_tok)):
                    dve.wait_ge(tok_done, 4 * p + n + 3)
                    dve.tensor_copy(dst[:], sq4(bank[n][:])).then_inc(tok_by_dve, 1)
                if not last:
                    split(2)
                for h in range(2):
                    for n, (dst, mask) in enumerate(((ab, "strict64"), (ak, "strict64"), (rb, "causal64"), (rk, "causal64"))):
                        dve.wait_ge(mats_done, 8 * p + 4 * h + n + 1)
                        tt(dst[:, h], sq4(bank[MAT_BANK[4 * h + n]][:]), const(mask), ALU.mult).then_inc(mats_ready, 1)
                    dve.wait_ge(mats_ready, 8 * p + 4 * h + 1)
                    order.done(tt(xt[:, h], ab[:, h], const("step1"), ALU.mult))
                    order.wait()
                    tt(xt[:, h], xt[:, h], const("ident"), ALU.add).then_inc(xt_ready, 1)
                for lv, size in enumerate(LEVELS):
                    for h in range(2):
                        dve.wait_ge(t_done, 10 * p + 2 * lv + h + 1)
                        tt(t_mat[:, h], sq4(bank[h][:]), const(f"step{size}"), ALU.mult).then_inc(t_ready, 1)
                    for h in range(2):
                        dve.wait_ge(xmul_done, 10 * p + 2 * lv + h + 1)
                        tt(xt[:, h], xt[:, h], sq4(bank[2 + h][:]), ALU.add).then_inc(xt_ready, 1)
                    if not last and lv == 1:
                        split(3)
                if not last:
                    split(4)
                dve.wait_ge(tail_ready, 3 * p + 3)
                order.done(dve.memset(state[0][:], 0.0))
                order.wait()
                dve.sem_inc(s_zero, 1)
                for c in range(N_CHUNKS):
                    t, ro = c // 2, HALF * (c % 2)
                    dve.wait_ge(u_done, N_CHUNKS * p + c + 1)
                    tt(u_tok[ro:ro + HALF, t, :], w_tok[ro:ro + HALF, t, :], bank[3][ro:ro + HALF, 0:P],
                       ALU.add).then_inc(u_ready, 1)
                    if c == N_CHUNKS - 1:
                        break
                    dve.wait_ge(s_done, (N_CHUNKS - 1) * p + c + 1)
                    if c:
                        dve.wait_ge(s_ready, (N_CHUNKS - 1) * p + c)
                    for h in range(2):
                        b = slice(HALF * h, HALF * h + HALF)
                        ins = dve.scalar_tensor_tensor(state[(c + 1) % 2][b, b], state[c % 2][b, b], g_last[b, c:c + 1],
                                                       bank[4][b, b], ALU.mult, ALU.add)
                    ins.then_inc(s_ready, 1)
                if not last:
                    split(5)
                dve.wait_ge(bonus_sum, p + 1)
                order.done(tt(bonus[:], bank[2][:], v[:], ALU.mult))
                dve.wait_ge(mean_done, p + 1)
                dve.scalar_tensor_tensor(y_mid[:], bank[0][:], -1.0 / HALF, y_sb[:], ALU.mult, ALU.add).then_inc(y_centered, 1)
                dve.wait_ge(y_rs, p + 2)
                order.done(tt(y_mid[:], y_mid[:], g_rs[:], ALU.mult))
                order.wait()
                order.done(dve.tensor_scalar(y_mid[:], y_mid[:], cols[:, LN_W, :], cols[:, LN_B, :], ALU.mult, ALU.add))
                order.wait()
                order.done(tt(y_mid[:], y_mid[:], bonus[:], ALU.add))
                order.wait()
                tt(y_out[:], y_mid[:], g[:], ALU.mult).then_inc(y_ready, 1)
                assert order.n == DVE_STEPS, order.n

            dve.wait_ge(z_read[0], 4)
            dve.wait_ge(z_read[1], 4)
            with dve.Fori(0, PAIRS // 2 - 1) as j:
                for q in range(2):
                    pair(2 * j + q, q, j, False)
            for q in range(2):
                pair(PAIRS - 2 + q, q, PAIRS // 2 - 1, q == 1)

        @block.tensor
        def _(pe):
            ident = keep["const"][:, CONST["ident"], :]
            block64 = keep["const"][:, CONST["block64"], :]
            pe.sem_inc(ring["unit_done"], 2)
            pe.sem_inc(lora_done, 3)

            def whole_unit(m, slot, count):
                ring_ready(pe, ring, m)
                pe.wait_ge(z_read[slot], count)
                for n in range(PASSES * KT):
                    mm = dense_pass(pe, z[slot][:], ring, slot, keep["xn_hi"], keep["xn_lo"], n)
                mm.then_inc(ring["unit_done"], 1)

            for m in range(FIRST):
                whole_unit(m, m % 2, m // 2 + 1)

            def pair(p, q, half, last):
                m = FIRST + UNITS * p
                total = PASSES * KT * (HG_GATES if last else UNITS)
                at_n = [0]

                def dense(count):
                    for _ in range(min(count, total - at_n[0])):
                        u, n = at_n[0] // (PASSES * KT), at_n[0] % (PASSES * KT)
                        slot = (q + u) % 2
                        if n == 0:
                            ring_ready(pe, ring, m + u)
                            pe.wait_ge(z_read[slot], UNITS * half + (FIRST + UNITS * q + u) // 2 + 1)
                        mm = dense_pass(pe, z[slot][:], ring, slot, keep["xn_hi"], keep["xn_lo"], n)
                        if n == PASSES * KT - 1:
                            mm.then_inc(ring["unit_done"], 1)
                        at_n[0] += 1

                tile = lambda t: slice(t * P, (t + 1) * P)
                pe.wait_ge(lora_in, 64 * p + 64)
                pe.wait_ge(low_ready, 3)
                pe.wait_ge(y_rs, p + 1)
                pe.matmul(bank[0][:], w_wa[0:HALF, :], low[0][0:HALF, :], start=True, stop=True).then_inc(lora_done, 1)
                pe.matmul(bank[1][:], w_wa[HALF:P, :], low[0][HALF:P, :], start=True, stop=True).then_inc(lora_done, 1)
                pe.matmul(bank[2][:], w_g1[:], low[1][:], start=True, stop=False)
                pe.matmul(bank[2][:], w_g2[:], low[2][:], start=False, stop=True).then_inc(lora_done, 1)
                dense(42)
                pe.wait_ge(kk_sq, p + 1)
                pe.matmul(bank[3][:], block64, sq[:], start=True, stop=True).then_inc(kk_sum, 1)
                dense(38)
                pe.wait_ge(operands_ready, 2 * p + 2)
                for b, src in ((4, v), (5, at), (0, bd), (1, kd)):
                    for t in range(TT):
                        mm = pe.transpose(bank[b][:, tile(t)], src[:, tile(t)], ident)
                    mm.then_inc(tok_done, 1)
                for h in range(2):
                    rows = slice(HALF * h, HALF * h + HALF)
                    for n, (lhs, rhs) in enumerate(((bt, at), (kt, at), (bt, rt), (kt, rt))):
                        b = MAT_BANK[4 * h + n]
                        if h == 0 and n == 0:
                            pe.wait_ge(g_ready, p + 1)
                        if h == 0 and n == 2:
                            pe.wait_ge(tok_by_act, 2 * p + 2)
                        if h == 1 and n == 0:
                            pe.wait_ge(tok_by_dve, 2 * p + 2)
                        if h == 1 and n >= 2:
                            pe.wait_ge(mats_ready, 8 * p + n - 1)
                        for t in range(TT):
                            mm = pe.matmul(bank[b][:, tile(t)], lhs[rows, tile(t)], rhs[rows, tile(t)], start=True, stop=True)
                        mm.then_inc(mats_done, 1)
                    dense(6)
                for h in range(2):
                    pe.wait_ge(mats_ready, 8 * p + (4 if h == 0 else 5))
                    for t in range(TT):
                        mm = pe.transpose(bank[4 + h][:, tile(t)], ab[:, h, t, :], ident)
                    mm.then_inc(a_done, 1)
                dense(6)
                for lv in range(len(LEVELS)):
                    for h in range(2):
                        pe.wait_ge(xt_ready, 12 * p + 2 * lv + h + 1)
                        if lv == 0:
                            pe.wait_ge(a_ready, 2 * p + h + 1)
                        for t in range(TT):
                            mm = pe.transpose(bank[4 + h][:, tile(t)], xt[:, h, t, :], ident)
                        mm.then_inc(xtr_done, 1)
                        for t in range(TT):
                            mm = pe.matmul(bank[h][:, tile(t)], a_mat[:, h, t, :], xt[:, h, t, :], start=True, stop=True)
                        mm.then_inc(t_done, 1)
                    dense(8)
                    for h in range(2):
                        pe.wait_ge(t_ready, 10 * p + 2 * lv + h + 1)
                        pe.wait_ge(x_ready, 10 * p + 2 * lv + h + 1)
                        for t in range(TT):
                            mm = pe.matmul(bank[2 + h][:, tile(t)], x_mat[:, h, t, :], t_mat[:, h, t, :], start=True, stop=True)
                        mm.then_inc(xmul_done, 1)
                    dense(6)
                for h in range(2):
                    f = slice(HALF * h, HALF * h + HALF)
                    for t in range(TT):
                        mm = pe.matmul(bank[0][:, t * P + HALF * h:t * P + HALF * h + HALF], ak[:, h, t, :], v_tok[:, t, f],
                                       start=True, stop=True)
                mm.then_inc(tail_done, 1)
                pe.wait_ge(xt_ready, 12 * p + 12)
                pe.wait_ge(tail_ready, 3 * p + 1)
                for h in range(2):
                    f = slice(HALF * h, HALF * h + HALF)
                    for t in range(TT):
                        mm = pe.matmul(bank[1][:, t * P + HALF * h:t * P + HALF * h + HALF], xt[:, h, t, :], akv[:, t, f],
                                       start=True, stop=True)
                mm.then_inc(tail_done, 1)
                for h in range(2):
                    f = slice(HALF * h, HALF * h + HALF)
                    for t in range(TT):
                        mm = pe.matmul(bank[2][f, tile(t)], a_tok[:, t, f], xt[:, h, t, :], start=True, stop=True)
                mm.then_inc(tail_done, 1)
                dense(4)
                pe.wait_ge(tail_ready, 3 * p + 3)
                pe.wait_ge(s_zero, p + 1)
                for c in range(N_CHUNKS):
                    t, ro = c // 2, HALF * (c % 2)
                    rows = slice(ro, ro + HALF)
                    s = slice(RW_CHUNK * c, RW_CHUNK * (c + 1))
                    if c:
                        pe.wait_ge(s_ready, (N_CHUNKS - 1) * p + c)
                    pe.matmul(bank[3][rows, 0:P], a_inv[:, s], state[c % 2][:], start=True, stop=True).then_inc(u_done, 1)
                    pe.matmul(bank[5][:, s], state[c % 2][:], rt[:, s], start=(c % 2 == 0), stop=False, skip_group_check=True)
                    pe.wait_ge(u_ready, N_CHUNKS * p + c + 1)
                    if c < N_CHUNKS - 1:
                        pe.matmul(bank[4][:, 0:P], k_tok[rows, t, :], v_tok[rows, t, :], start=True, stop=False)
                        pe.matmul(bank[4][:, 0:P], b_tok[rows, t, :], u_tok[rows, t, :], start=False,
                                  stop=True).then_inc(s_done, 1)
                    if c % 2:
                        for h in range(2):
                            f = slice(HALF * h, HALF * h + HALF)
                            pe.matmul(bank[5][f, tile(t)], v_tok[:, t, f], rk[:, h, t, :], start=False, stop=False,
                                      skip_group_check=True)
                            mm = pe.matmul(bank[5][f, tile(t)], u_tok[:, t, f], rb[:, h, t, :], start=False, stop=True,
                                           skip_group_check=True)
                        if c == N_CHUNKS - 1:
                            mm.then_inc(y_done, 1)
                    dense(4)
                pe.matmul(bank[2][:], block64, bonus[:], start=True, stop=True).then_inc(bonus_sum, 1)
                dense(6)
                pe.wait_ge(y_copied, p + 1)
                pe.matmul(bank[0][:], block64, y_sb[:], start=True, stop=True).then_inc(mean_done, 1)
                dense(12)
                pe.wait_ge(y_sq, p + 1)
                pe.matmul(bank[1][:], block64, sq[:], start=True, stop=True).then_inc(var_done, 1)
                dense(total)

            with pe.Fori(0, PAIRS // 2 - 1) as j:
                for q in range(2):
                    pair(2 * j + q, q, j, False)
            for q in range(2):
                pair(PAIRS - 2 + q, q, PAIRS // 2 - 1, q == 1)


def phase_merge(nc, io, keep):
    N_OUT = 4
    NB = D // N_OUT
    w_hg, w_rw = k_tiles(io["w_branch_hg"][0]), k_tiles(io["w_branch_rw"][0])
    w_out = k_tiles(io["w_out"][0])
    with ExitStack() as ctx:
        mem = Memory(nc, ctx)
        y_lo, m_lo = (mem.sb(n, [P, KT, T], F32R) for n in ("y_lo", "merged_lo"))
        y_raw, m_hi = mem.shared(("y_raw", [P, KT, T], F32), ("merged_hi", [P, KT, T], F32R))
        y_hi, h = keep["y_hi"], keep["h"]
        ring = make_ring(mem, "mg")
        gates = [mem.sb(f"mg_gates{s}", [P, 2, T]) for s in range(2)]
        part_h, part_r, merged = (mem.sb(n, [P, T]) for n in ("part_hg", "part_rw", "merged"))
        z = [[mem.psum(f"mg_z{s}{b}", [P, T]) for b in range(2)] for s in range(2)]
        out = [mem.psum(f"mg_out{t}", [P, NB]) for t in range(TT)]
        y_in = mem.sem("mg_y_in0", "mg_y_in1", "mg_y_in2", "mg_y_in3")
        y_part = lambda n: y_raw[:, 4 * n:4 * n + 4, :]
        gates_in = mem.sem("gates_in0", "gates_in1")
        y_hi_done, y_lo_done, parts, sum_ready, sum_hi, sum_lo = mem.sem(
            "y_hi_done", "y_lo_done", "mg_parts", "sum_ready", "sum_hi", "sum_lo")
        x_in, h_ready, group_done, branches_done, squares = mem.sem(
            "res_x_in", "h_ready", "group_done", "branches_done", "h_squares")
        tile4 = lambda a: a[:].rearrange("p k c -> p (k c)").rearrange("p (a t) -> p a t", t=T)
        half = KT // 2
        block = ctx.enter_context(nc.Block())

        @block.sync
        def _(sp):
            for n in range(4):
                src = io["y_hg" if n < 2 else "y_rw"][4 * (n % 2):4 * (n % 2) + 4].rearrange("a p t -> p a t")
                sp.dma_start(y_part(n), src).then_inc(y_in[n], 16)
            with sp.Fori(0, KT // 2) as j:
                for q in range(2):
                    f = 2 * j + q
                    wait_apart(sp, ring["passed"], ring["lo_done"], f + 1)
                    cols = bass.ds(P * f, P)
                    sp.dma_start(ring["raw"][q][:, 0:half, :], w_hg[:, :, cols]).then_inc(ring["raw_in"][q], 16)
                    sp.dma_start(ring["raw"][q][:, half:KT, :], w_rw[:, :, cols]).then_inc(ring["raw_in"][q], 16)
                    wait_apart(sp, ring["passed"], parts, f + 1)
                    src = io["gate"].rearrange("(b f) p t -> f p b t", b=2)[bass.ds(f, 1)].rearrange("a p b t -> p (a b) t")
                    sp.dma_start(gates[q][:], src).then_inc(gates_in[q], 16)
            with sp.Fori(0, N_OUT) as j:
                for kq in range(4):
                    wait_apart(sp, ring["passed"], ring["lo_done"], KT + 4 * j + kq + 1)
                    for k in (0, 2):
                        sp.dma_start(tile4(ring["raw"][kq % 2])[:, k:k + 2, :],
                                     w_out[:, 4 * kq + k:4 * kq + k + 2, bass.ds(NB * j, NB)]).then_inc(ring["raw_in"][kq % 2], 16)

        @block.gpsimd
        def _(pool):
            pool.wait_ge(branches_done, 1)
            for t in range(TT):
                pool.dma_start(h[:, t, :], io["x"][0][t * P:(t + 1) * P, :]).then_inc(x_in, 16)

        @block.scalar
        def _(act):
            def hi(m, slot, landed):
                act.wait_ge(ring["raw_in"][slot], landed)
                act.wait_ge(ring["unit_done"], m + 1)
                act.activation(ring["hi"][slot][:], ring["raw"][slot][:], ACT.Copy).then_inc(ring["hi_done"], 1)

            for n in range(4):
                act.wait_ge(y_in[n], 16)
                act.activation(y_hi[:, 4 * n:4 * n + 4, :], y_part(n), ACT.Copy).then_inc(y_hi_done, 1)
            hi(0, 0, 32)
            with act.Fori(0, KT // 2) as j:
                for q in range(2):
                    f = 2 * j + q
                    hi(f + 1, (q + 1) % 2, 32 * j + 32 + 32 * q)
                    act.wait_ge(sum_ready, f + 1)
                    act.activation(m_hi[:, bass.ds(f, 1), :].rearrange("p a t -> p (a t)"), merged[:],
                                   ACT.Copy).then_inc(sum_hi, 1)

            def group(j, more):
                for kq in range(4 if more else 3):
                    hi(KT + 4 * j + kq + 1, (kq + 1) % 2, 32 * (KT // 2) + 64 * j + 32 * ((kq + 1) // 2) + 32)
                for t in range(TT):
                    act.wait_ge(h_ready, 4 * j + t + 1)
                    act.wait_ge(squares, 4 * j + t + 1)
                    act.activation(merged[:], h[:, t, bass.ds(NB * j, NB)], ACT.Square,
                                   accum_out=keep["h_squares"][:, t, bass.ds(j, 1)]).then_inc(squares, 1)

            act.sem_inc(squares, 1)
            with act.Fori(0, N_OUT - 1) as j:
                group(j, True)
            group(N_OUT - 1, False)

        @block.vector
        def _(dve):
            dve.sem_inc(ring["lo_done"], 2)
            dve.sem_inc(parts, 2)
            for n in range(4):
                dve.wait_ge(y_hi_done, n + 1)
                dve.tensor_tensor(y_lo[:, 4 * n:4 * n + 4, :], y_part(n),
                                  y_hi[:, 4 * n:4 * n + 4, :].bitcast(F32), ALU.subtract).then_inc(y_lo_done, 1)
            ring_lo(dve, ring, 0, 0)
            with dve.Fori(0, KT // 2) as j:
                for q in range(2):
                    f = 2 * j + q
                    ring_lo(dve, ring, (q + 1) % 2, f + 1)
                    ring_used(dve, ring, f)
                    dve.wait_ge(gates_in[q], 16 * j + 16)
                    dve.tensor_tensor(part_h[:], z[q][0][:], gates[q][:, 0, :], ALU.mult)
                    dve.tensor_tensor(part_r[:], z[q][1][:], gates[q][:, 1, :], ALU.mult).then_inc(parts, 1)
                    dve.wait_ge(parts, f + 3)
                    dve.tensor_tensor(merged[:], part_h[:], part_r[:], ALU.add).then_inc(sum_ready, 1)
                    dve.wait_ge(sum_hi, f + 1)
                    one = lambda a: a[:, bass.ds(f, 1), :].rearrange("p a t -> p (a t)")
                    dve.tensor_tensor(one(m_lo), merged[:], one(m_hi).bitcast(F32), ALU.subtract).then_inc(sum_lo, 1)
            dve.wait_ge(parts, KT + 2)
            dve.sem_inc(branches_done, 1)

            def group(j, more):
                for kq in range(4 if more else 3):
                    ring_lo(dve, ring, (kq + 1) % 2, KT + 4 * j + kq + 1)
                dve.wait_ge(x_in, 16 * TT)
                for t in range(TT):
                    dve.wait_ge(group_done, 4 * j + t + 1)
                    b = h[:, t, bass.ds(NB * j, NB)]
                    dve.tensor_tensor(b, out[t][:], b, ALU.add).then_inc(h_ready, 1)

            with dve.Fori(0, N_OUT - 1) as j:
                group(j, True)
            group(N_OUT - 1, False)

        @block.tensor
        def _(pe):
            pe.sem_inc(ring["unit_done"], 2)
            pe.wait_ge(y_lo_done, 4)
            with pe.Fori(0, KT // 2) as j:
                for q in range(2):
                    f = 2 * j + q
                    ring_ready(pe, ring, f)
                    pe.wait_ge(parts, f + 1)
                    for k in range(KT):
                        mm = product(pe, z[q][k // half][:], ring["hi"][q][:, k, :], ring["lo"][q][:, k, :], y_hi[:, k, :],
                                     y_lo[:, k, :], k % half == 0, k % half == half - 1)
                    mm.then_inc(ring["unit_done"], 1)
            pe.wait_ge(sum_lo, KT)

            def group(j, first):
                for kq in range(4):
                    ring_ready(pe, ring, KT + 4 * j + kq)
                    w_h, w_l = tile4(ring["hi"][kq % 2]), tile4(ring["lo"][kq % 2])
                    for t in range(TT):
                        if kq == 0 and not first:
                            pe.wait_ge(h_ready, 4 * (j - 1) + t + 1)
                        s = slice(t * P, (t + 1) * P)
                        for k in range(4):
                            a, last = 4 * kq + k, kq == 3 and k == 3
                            pe.matmul(out[t][:], m_hi[:, a, s], w_h[:, k, :], start=(a == 0), stop=False, skip_group_check=True)
                            pe.matmul(out[t][:], m_hi[:, a, s], w_l[:, k, :], start=False, stop=False, skip_group_check=True)
                            mm = pe.matmul(out[t][:], m_lo[:, a, s], w_h[:, k, :], start=False, stop=last,
                                           skip_group_check=True)
                        if kq == 3:
                            mm.then_inc(group_done, 1)
                    if kq < 3:
                        mm.then_inc(ring["unit_done"], 1)
                    else:
                        pe.wait_ge(group_done, 4 * j + 4)
                        pe.sem_inc(ring["unit_done"], 1)

            group(0, True)
            with pe.Fori(1, N_OUT) as j:
                group(j, False)


def phase_route(nc, io, keep):
    NL = N_GROUPS + N_EXPERTS
    PG, E = PER_GROUP, N_EXPERTS
    with ExitStack() as ctx:
        mem = Memory(nc, ctx)
        h, hn = keep["h"], mem.sb("hn", [P, TT, D])
        hn_t = mem.sb("hn_t", [P, KT, T])
        w_bc = mem.sb("ffn_norm_rows", [P, D])
        w_r = mem.sb("w_router", [P, KT, NL])
        bias = mem.sb("router_bias", [1, NL])
        var, rstd, tmp = (mem.sb("h_" + n, [P, TT]) for n in ("var", "rstd", "rstd_tmp"))
        lg, lg_t = mem.sb("logits", [P, TT, NL]), mem.sb("logits_t", [NL, T])
        one = lambda n: mem.sb("rt_" + n, [P, TT, 1])
        eight = lambda n: mem.sb("rt_" + n, [P, TT, PG])
        gmax, gsum, p_group, best, second, ratio, first_at, denom = (one(n) for n in (
            "gmax", "gsum", "p_group", "best", "second", "ratio", "first_at", "denom"))
        eq, sel_g, cand, el, part, sel1, sel2 = (eight(n) for n in ("eq", "sel_g", "cand", "el", "part", "sel1", "sel2"))
        m1, m2, m12, slot_e, prod = (mem.sb("rt_" + n, [P, TT, E]) for n in ("m1", "m2", "m12", "slot_e", "prod"))
        count, blocks, ends, start, slot_f = (mem.sb("rt_" + n, sh) for n, sh in (
            ("count", [P, E]), ("blocks", [P, E]), ("ends", [P, E]), ("start", [P, E]), ("slot_f", [P, 2, TT])))
        over, after = mem.sb("rt_over", [P, E, PG]), mem.sb("rt_after", [1, MAX_BLOCKS + 2, E])
        blk_f = mem.sb("rt_blk_f", [1, MAX_BLOCKS + 2])
        total = mem.sb("rt_total", [1, 1])
        tok_f, tok_id = mem.sb("rt_tok_f", [P, TT]), mem.sb("rt_tok_id", [P, TT], U32)
        zero = mem.sb("rt_zero", [TABLE_BLOCKS, SLOTS], U32)
        tr = [mem.psum(f"h_tr{b}", [P, T]) for b in range(4)]
        lgt_ps = mem.psum("lgt_ps", [NL, T])
        lg_ps, rank_ps, count_ps = mem.psum("lg_ps", [P, TT, NL]), mem.psum("rank_ps", [P, TT, E]), mem.psum("count_ps", [P, E])
        w_in_, root_done, dve_o, scaled, hn_stored, turned, tr_read, lgt_done, lgt_read = mem.sem(
            "router_in", "h_root_done", "rt_dve_o", "hn_scaled", "hn_stored", "h_turned", "h_tr_read", "lgt_done", "lgt_read")
        var_ready, lg_done, diff_ready, exp_done, mask_ready, rank_done, slots_ready, zeroed, table_zero, scattered = mem.sem(
            "var_ready", "lg_done", "diff_ready", "rt_exp_done", "mask_ready", "rank_done", "slots_ready", "rt_zeroed",
            "table_zero", "scattered")
        ramp = keep["const"][:, CONST["ramp"], :]
        block = ctx.enter_context(nc.Block())

        @block.sync
        def _(sp):
            sp.dma_start(w_bc[:], io["norm_ffn_w"].to_broadcast([P, D])).then_inc(w_in_, 16)
            sp.dma_start(w_r[:, :, 0:N_GROUPS], k_tiles(io["router_group_w"][0])).then_inc(w_in_, 16)
            sp.dma_start(w_r[:, :, N_GROUPS:NL], k_tiles(io["router_expert_w"][0])).then_inc(w_in_, 16)
            sp.dma_start(bias[:, 0:N_GROUPS], io["router_group_b"]).then_inc(w_in_, 16)
            sp.dma_start(bias[:, N_GROUPS:NL], io["router_expert_b"]).then_inc(w_in_, 16)
            for t in range(TT):
                sp.wait_ge(scaled, t + 1)
                sp.dma_start(io["hn"][t * P:(t + 1) * P, :], hn[:, t, :]).then_inc(hn_stored, 16)
            sp.wait_ge(hn_stored, 16 * TT)

        @block.gpsimd
        def _(pool):
            pool.memset(zero[:], 0).then_inc(zeroed, 1)
            pool.wait_ge(zeroed, 1)
            pool.dma_start(io["slot_tok"].rearrange("(a b) c -> a (b c)", b=SLOTS), zero[:]).then_inc(table_zero, 16)
            pool.wait_ge(table_zero, 16)
            pool.wait_ge(slots_ready, 1)
            for t in range(TT):
                for c in range(2):
                    pool.indirect_dma_start(io["slot_tok"], bass.IndirectOffsetOnAxis(ap=keep["slots"][:, c, t:t + 1], axis=0),
                                            tok_id[:, t:t + 1], None).then_inc(scattered, 16)
            pool.wait_ge(scattered, 16 * 2 * TT)

        @block.scalar
        def _(act):
            act.wait_ge(var_ready, 1)
            act.activation(tmp[:], rstd[:], ACT.Sqrt).then_inc(root_done, 1)
            for n in range(4 * TT):
                t, g = n // 4, n % 4
                act.wait_ge(turned, n + 1)
                act.activation(hn_t[:, 4 * g:4 * g + 4, t * P:(t + 1) * P], tr[g][:].rearrange("p (k c) -> p k c", c=P),
                               ACT.Copy).then_inc(tr_read, 1)
            act.wait_ge(lgt_done, 1)
            act.activation(lg_t[:], lgt_ps[:], ACT.Copy).then_inc(lgt_read, 1)
            act.wait_ge(diff_ready, 1)
            act.activation(cand[:, :, 0:N_GROUPS], cand[:, :, 0:N_GROUPS], ACT.Exp).then_inc(exp_done, 1)
            act.wait_ge(diff_ready, 2)
            act.activation(ratio[:], ratio[:], ACT.Exp).then_inc(exp_done, 1)

        @block.vector
        def _(dve):
            order = Order(dve, dve_o)
            tt, ts = dve.tensor_tensor, dve.tensor_scalar

            def step(ins):
                order.done(ins)
                order.wait()

            step(dve.tensor_reduce(var[:], keep["h_squares"][:], AX_X, ALU.add))
            ts(rstd[:], var[:], 1.0 / D, NORM_EPS, ALU.mult, ALU.add).then_inc(var_ready, 1)
            dve.wait_ge(root_done, 1)
            step(dve.reciprocal(var[:], tmp[:]))
            step(tt(tmp[:], var[:], var[:], ALU.mult))
            step(tt(tmp[:], tmp[:], rstd[:], ALU.mult))
            step(ts(tmp[:], tmp[:], -0.5, 1.5, ALU.mult, ALU.add))
            step(tt(rstd[:], tmp[:], var[:], ALU.mult))
            dve.wait_ge(w_in_, 16 * 5)
            for t in range(TT):
                dve.scalar_tensor_tensor(hn[:, t, :], h[:, t, :], rstd[:, t:t + 1], w_bc[:], ALU.mult,
                                         ALU.mult).then_inc(scaled, 1)
            dve.wait_ge(lg_done, 1)
            step(dve.tensor_copy(lg[:], lg_ps[:]))
            bc = lambda a, n: a.to_broadcast([P, TT, n])
            ramp4 = lambda n: ramp[:, 0:n].rearrange("p (a g) -> p a g", a=1).to_broadcast([P, TT, n])

            def choose(sel, values, top, n):
                step(dve.tensor_reduce(top[:], values, AX_X, ALU.max))
                step(tt(eq[:, :, 0:n], values, bc(top[:], n), ALU.is_equal))
                step(ts(eq[:, :, 0:n], eq[:, :, 0:n], -float(P), float(P), ALU.mult, ALU.add))
                step(tt(eq[:, :, 0:n], eq[:, :, 0:n], ramp4(n), ALU.add))
                step(dve.tensor_reduce(first_at[:], eq[:, :, 0:n], AX_X, ALU.min))
                step(tt(sel[:, :, 0:n], ramp4(n), bc(first_at[:], n), ALU.is_equal))

            groups = lg[:, :, 0:N_GROUPS]
            choose(sel_g, groups, gmax, N_GROUPS)
            tt(cand[:, :, 0:N_GROUPS], groups, bc(gmax[:], N_GROUPS), ALU.subtract).then_inc(diff_ready, 1)
            dve.wait_ge(exp_done, 1)
            step(dve.tensor_reduce(gsum[:], cand[:, :, 0:N_GROUPS], AX_X, ALU.add))
            step(dve.reciprocal(p_group[:], gsum[:]))
            for g in range(N_GROUPS):
                src = lg[:, :, N_GROUPS + PG * g:N_GROUPS + PG * (g + 1)]
                step(tt((el if g == 0 else part)[:], src, bc(sel_g[:, :, g:g + 1], PG), ALU.mult))
                if g:
                    step(tt(el[:], el[:], part[:], ALU.add))
            choose(sel1, el[:], best, PG)
            step(dve.scalar_tensor_tensor(cand[:], sel1[:], -3.0e38, el[:], ALU.mult, ALU.add))
            choose(sel2, cand[:], second, PG)
            tt(ratio[:], second[:], best[:], ALU.subtract).then_inc(diff_ready, 1)
            dve.wait_ge(exp_done, 2)
            step(ts(denom[:], ratio[:], 1.0, None, ALU.add))
            step(dve.reciprocal(gmax[:], denom[:]))
            wts = keep["weights"]
            step(tt(wts[:, 0, :], p_group[:, :, 0], gmax[:, :, 0], ALU.mult))
            step(tt(wts[:, 1, :], wts[:, 0, :], ratio[:, :, 0], ALU.mult))
            for g in range(N_GROUPS):
                s = slice(PG * g, PG * (g + 1))
                tt(m1[:, :, s], sel1[:], bc(sel_g[:, :, g:g + 1], PG), ALU.mult)
                last = tt(m2[:, :, s], sel2[:], bc(sel_g[:, :, g:g + 1], PG), ALU.mult)
            step(last)
            tt(m12[:], m1[:], m2[:], ALU.add).then_inc(mask_ready, 1)
            dve.wait_ge(rank_done, 1)
            step(dve.tensor_copy(count[:], count_ps[:]))
            step(ts(over[:], ramp[:, 0:PG].rearrange("p (a g) -> p a g", a=1).to_broadcast([P, E, PG]), float(SLOTS), None,
                    ALU.mult))
            step(tt(over[:], count[:].rearrange("p (e a) -> p e a", a=1).to_broadcast([P, E, PG]), over[:], ALU.is_gt))
            step(dve.tensor_reduce(blocks[:], over[:], AX_X, ALU.add))
            step(dve.memset(start[:], 1.0))
            step(dve.tensor_tensor_scan(ends[:], start[:], blocks[:], 0.0, ALU.mult, ALU.add))
            step(tt(start[:], ends[:], blocks[:], ALU.subtract))
            step(ts(start[:], start[:], float(SLOTS), None, ALU.mult))
            step(tt(slot_e[:], rank_ps[:], start[:].rearrange("p (a e) -> p a e", a=1).to_broadcast([P, TT, E]), ALU.add))
            for c, m in enumerate((m1, m2)):
                step(tt(prod[:], m[:], slot_e[:], ALU.mult))
                step(dve.tensor_reduce(slot_f[:, c, :], prod[:], AX_X, ALU.add))
            step(dve.tensor_copy(keep["slots"][:], slot_f[:]))
            for t in range(TT):
                last = ts(tok_f[:, t:t + 1], ramp[:, P - 1:P], float(P * t), None, ALU.add)
            step(last)
            dve.tensor_copy(tok_id[:], tok_f[:]).then_inc(slots_ready, 1)
            nb = MAX_BLOCKS + 2
            step(tt(after[:], ends[0:1, :].rearrange("p (a e) -> p a e", a=1).to_broadcast([1, nb, E]),
                    ramp[0:1, 0:nb].rearrange("p (b a) -> p b a", a=1).to_broadcast([1, nb, E]), ALU.is_le))
            step(dve.tensor_reduce(blk_f[:], after[:], AX_X, ALU.add))
            step(ts(blk_f[:], blk_f[:], float(E - 1), None, ALU.min))
            step(dve.tensor_copy(keep["blk_expert"][:], blk_f[:]))
            nj = MAX_BLOCKS // 2
            step(ts(blk_f[:, 0:nj], ramp[0:1, 0:nj], 2.0, None, ALU.mult))
            step(tt(blk_f[:, 0:nj], ends[0:1, E - 1:E].to_broadcast([1, nj]), blk_f[:, 0:nj], ALU.is_gt))
            step(dve.tensor_reduce(total[:], blk_f[:, 0:nj], AX_X, ALU.add))
            step(ts(total[:], total[:], 2.0, None, ALU.mult))
            step(dve.tensor_copy(keep["n_blocks"][:], total[:]))

        @block.tensor
        def _(pe):
            ident, ones = keep["const"][:, CONST["ident"], :], keep["const"][:, CONST["ones"], :]
            pe.wait_ge(w_in_, 16 * 5)

            def turn(t):
                pe.wait_ge(scaled, t + 1)
                for g in range(4):
                    if t:
                        pe.wait_ge(tr_read, 4 * (t - 1) + g + 1)
                    for k in range(4):
                        f = (4 * g + k) * P
                        mm = pe.transpose(tr[g][:, k * P:(k + 1) * P], hn[:, t, f:f + P], ident)
                    mm.then_inc(turned, 1)

            turn(0)
            for t in range(TT):
                if t + 1 < TT:
                    turn(t + 1)
                pe.wait_ge(tr_read, 4 * t + 4)
                tile = slice(t * P, (t + 1) * P)
                pe.matmul(lgt_ps[:, tile], bias[:], ones[0:1, :], start=True, stop=False, skip_group_check=True)
                for k in range(KT):
                    mm = pe.matmul(lgt_ps[:, tile], w_r[:, k, :], hn_t[:, k, tile], start=False, stop=(k == KT - 1),
                                   skip_group_check=True)
            mm.then_inc(lgt_done, 1)
            pe.wait_ge(lgt_read, 1)
            for t in range(TT):
                mm = pe.transpose(lg_ps[:, t, :], lg_t[:, t * P:(t + 1) * P], ident[0:NL, 0:NL])
            mm.then_inc(lg_done, 1)
            pe.wait_ge(mask_ready, 1)
            for t in range(TT):
                mm = pe.matmul(rank_ps[:, t, :], keep["const"][:, CONST["prefix"], :], m12[:, t, :], start=True,
                               stop=(t == 0), skip_group_check=True)
                for b in range(t):
                    mm = pe.matmul(rank_ps[:, t, :], ones, m12[:, b, :], start=False, stop=(b == t - 1), skip_group_check=True)
            for t in range(TT):
                mm = pe.matmul(count_ps[:], ones, m12[:, t, :], start=(t == 0), stop=(t == TT - 1))
            mm.then_inc(rank_done, 1)



def phase_experts(nc, io, keep):
    UPS, GATES, DOWNS = range(0, 4), range(4, 8), range(8, 12)
    UNITS, DEPTH, AHEAD = 12, 4, 2
    DC = D_EXPERT // P
    with ExitStack() as ctx:
        mem = Memory(nc, ctx)
        ring = make_ring(mem, "ex", (4, D_EXPERT), DEPTH)
        idx = [mem.sb(f"ex_idx{s}", [SLOTS, 1], U32) for s in range(2)]
        xg = [mem.sb(f"ex_x{s}", [SLOTS, D]) for s in range(2)]
        x_hi, x_lo = ([mem.sb(f"ex_x_{n}{s}", [P, KT, SLOTS], F32R) for s in range(2)] for n in ("hi", "lo"))
        sig, act_g, h_sb = (mem.sb("ex_" + n, [SLOTS, D_EXPERT]) for n in ("sig", "act_g", "h"))
        h_hi, h_lo = (mem.sb(f"ex_h_{n}", [P, DC, SLOTS], F32R) for n in ("hi", "lo"))
        y_sb = [mem.sb(f"ex_y{s}", [SLOTS, D]) for s in range(2)]
        gate_ps = [mem.psum(f"ex_gate{s}", [SLOTS, D_EXPERT]) for s in range(2)]
        up_ps = mem.psum("ex_up", [SLOTS, D_EXPERT])
        down_ps = [mem.psum(f"ex_down{s}", [SLOTS, D_EXPERT]) for s in range(2)]
        x_ps = [mem.psum(f"ex_xt{g}", [P, KT // 2, SLOTS]) for g in range(2)]
        h_ps = mem.psum("ex_ht", [P, DC, SLOTS])
        idx_in = mem.sem("ex_idx_in")
        x_in = mem.sem("ex_x_in0", "ex_x_in1")
        x_turned, x_hi_done, x_ready, sig_ready, gated, h_done, h_turned, h_hi_done, h_ready = mem.sem(
            "ex_x_turned", "ex_x_hi_done", "ex_x_ready", "ex_sig_ready", "ex_gated", "ex_h_done", "ex_h_turned",
            "ex_h_hi_done", "ex_h_ready")
        y_read, y_stored, y_free = mem.sem("ex_y_read", "ex_y_stored", "ex_y_free")
        block = ctx.enter_context(nc.Block())

        def blocks(eng):
            return eng.value_load(keep["n_blocks"][:], min_val=2, max_val=MAX_BLOCKS)

        @block.sync
        def _(sp):
            def expert(b):
                return sp.value_load(keep["blk_expert"][0:1, bass.ds(b, 1)], min_val=0, max_val=N_EXPERTS - 1)

            def load(key, e, n, m, slot):
                w = io[key][0][bass.ds(e, 1)].rearrange("a (k p) n -> p (a k) n", p=P)
                src = w[:, :, D_EXPERT * n:D_EXPERT * (n + 1)] if key == "expert_w_down" else w[:, 4 * n:4 * n + 4, :]
                ring_load(sp, ring, slot, m, src)

            n_blocks = blocks(sp)
            e0 = expert(0)
            for n in range(4):
                if n == 2:
                    sp.wait_ge(x_in[0], 16)
                load("expert_w_gate", e0, n, n, n)
            with sp.Fori(0, n_blocks, 2) as i:
                for u in range(2):
                    b = i + u
                    m = 4 + UNITS * b
                    e, e_next = expert(b), expert(b + 1)
                    for n in range(4):
                        load("expert_w_up", e, n, m + UPS[n], n)
                    for n in range(4):
                        load("expert_w_gate", e_next, n, m + GATES[n], n)
                    for n in range(4):
                        load("expert_w_down", e, n, m + DOWNS[n], n)
            for n in range(AHEAD):
                load("expert_w_up", e0, n, 4 + UNITS * n_blocks + n, n)

        @block.gpsimd
        def _(pool):
            n_blocks = blocks(pool)

            def gather(b, s, count):
                pool.dma_start(idx[s][:], io["slot_tok"][bass.ds(SLOTS * b, SLOTS), :]).then_inc(idx_in, 16)
                wait_apart(pool, keep["pool_waits"], idx_in, count)
                pool.indirect_dma_start(xg[s][:], None, io["hn"], bass.IndirectOffsetOnAxis(ap=idx[s][:], axis=0)
                                        ).then_inc(x_in[s], 16)

            pool.sem_inc(y_free, 2)
            gather(0, 0, 16)
            gather(1, 1, 32)
            with pool.Fori(0, n_blocks, 2) as i:
                for u in range(2):
                    b = i + u
                    wait_apart(pool, keep["pool_waits"], x_turned, 2 * b + 2)
                    gather(b + 2, u, 16 * b + 48)
                    wait_apart(pool, keep["pool_waits"], y_read, 4 * b + 6)
                    pool.dma_start(io["ys"][bass.ds(SLOTS * b, SLOTS), :], y_sb[u][:]).then_inc(y_stored, 16)
                    pool.wait_ge(y_stored, 16 * b + 16)
                    pool.sem_inc(y_free, 1)

        @block.scalar
        def _(act):
            n_blocks = blocks(act)

            def output(b, u, n, m):
                if n == 0:
                    act.wait_ge(y_free, b + 1)
                ring_used(act, ring, m + DOWNS[n])
                act.activation(y_sb[u][:, D_EXPERT * n:D_EXPERT * (n + 1)], down_ps[n % 2][:], ACT.Copy).then_inc(y_read, 1)

            def x_high(s, turned):
                for g in range(2):
                    act.wait_ge(x_turned, turned + g + 1)
                    act.activation(x_hi[s][:, 8 * g:8 * g + 8, :], x_ps[g][:], ACT.Copy).then_inc(x_hi_done, 1)

            x_high(0, 0)
            for n in range(4):
                ring_hi(act, ring, n, n, 0)
            for n in range(AHEAD):
                ring_hi(act, ring, n, 4 + n, 1)
            with act.Fori(0, n_blocks, 2) as i:
                for u in range(2):
                    b = i + u
                    m = 4 + UNITS * b
                    for w in range(UNITS):
                        if w in (10, 11):
                            output(b, u, w - 10, m)
                        ring_hi(act, ring, (w + AHEAD) % 4, m + w + AHEAD, 1 + 3 * b + (w + AHEAD) // 4)
                        if w == 0:
                            x_high((u + 1) % 2, 2 * b + 2)
                            act.wait_ge(ring["unit_done"], m + DEPTH)
                            act.activation(sig[:], gate_ps[u][:], ACT.Sigmoid).then_inc(sig_ready, 1)
                        if w == 6:
                            act.wait_ge(h_turned, b + 1)
                            act.activation(h_hi[:], h_ps[:], ACT.Copy).then_inc(h_hi_done, 1)
                    output(b, u, 2, m)
                    output(b, u, 3, m)

        @block.vector
        def _(dve):
            n_blocks = blocks(dve)
            dve.sem_inc(ring["lo_done"], DEPTH)
            dve.sem_inc(h_done, 1)

            def x_low(s, turned):
                for g in range(2):
                    dve.wait_ge(x_hi_done, turned + g + 1)
                    dve.tensor_tensor(x_lo[s][:, 8 * g:8 * g + 8, :], x_ps[g][:], x_hi[s][:, 8 * g:8 * g + 8, :].bitcast(F32),
                                      ALU.subtract).then_inc(x_ready, 1)

            x_low(0, 0)
            for n in range(4):
                ring_lo(dve, ring, n, n)
            for n in range(AHEAD):
                ring_lo(dve, ring, n, 4 + n)
            with dve.Fori(0, n_blocks, 2) as i:
                for u in range(2):
                    b = i + u
                    m = 4 + UNITS * b
                    for w in range(UNITS):
                        ring_lo(dve, ring, (w + AHEAD) % 4, m + w + AHEAD)
                        if w == 0:
                            x_low((u + 1) % 2, 2 * b + 2)
                            dve.wait_ge(sig_ready, b + 1)
                            dve.tensor_tensor(act_g[:], gate_ps[u][:], sig[:], ALU.mult).then_inc(gated, 1)
                        if w == 5:
                            dve.wait_ge(gated, b + 1)
                            ring_used(dve, ring, m + UPS[3])
                            dve.tensor_tensor(h_sb[:], up_ps[:], act_g[:], ALU.mult).then_inc(h_done, 1)
                        if w == 6:
                            dve.wait_ge(h_hi_done, b + 1)
                            dve.tensor_tensor(h_lo[:], h_ps[:], h_hi[:].bitcast(F32), ALU.subtract).then_inc(h_ready, 1)

        @block.tensor
        def _(pe):
            ident = keep["const"][0:SLOTS, CONST["ident"], 0:SLOTS]
            n_blocks = blocks(pe)
            pe.sem_inc(ring["unit_done"], DEPTH)
            pe.sem_inc(y_read, 2)

            def turn_x(s, landed):
                wait_apart(pe, keep["pe_waits"], x_in[s], landed)
                for g in range(2):
                    for k in range(8):
                        f = (8 * g + k) * P
                        mm = pe.transpose(x_ps[g][:, k, :], xg[s][:, f:f + P], ident)
                    mm.then_inc(x_turned, 1)

            def multiply(out, a_hi, a_lo, first_k, slot, m, first, last):
                ring_ready(pe, ring, m)
                for k in range(4):
                    w_h, w_l = ring["hi"][slot][:, k, :], ring["lo"][slot][:, k, :]
                    a_h, a_l = a_hi[:, first_k + k, :], a_lo[:, first_k + k, :]
                    pe.matmul(out[:], a_h, w_h, start=(first and k == 0), stop=False, skip_group_check=True)
                    pe.matmul(out[:], a_h, w_l, start=False, stop=False, skip_group_check=True)
                    mm = pe.matmul(out[:], a_l, w_h, start=False, stop=(last and k == 3), skip_group_check=True)
                mm.then_inc(ring["unit_done"], 1)

            turn_x(0, 16)
            pe.wait_ge(x_ready, 2)
            for n in range(4):
                multiply(gate_ps[0], x_hi[0], x_lo[0], 4 * n, n, n, n == 0, n == 3)
            with pe.Fori(0, n_blocks, 2) as i:
                for u in range(2):
                    b = i + u
                    v = (u + 1) % 2
                    m = 4 + UNITS * b
                    turn_x(v, 8 * i + 16 + 16 * u)
                    pe.wait_ge(h_done, b + 1)
                    for n in range(4):
                        multiply(up_ps, x_hi[u], x_lo[u], 4 * n, n, m + UPS[n], n == 0, n == 3)
                    pe.wait_ge(x_ready, 2 * b + 4)
                    for n in range(4):
                        if n == 3:
                            wait_apart(pe, keep["pe_waits"], h_done, b + 2)
                            for k in range(DC):
                                mm = pe.transpose(h_ps[:, k, :], h_sb[:, k * P:(k + 1) * P], ident)
                            mm.then_inc(h_turned, 1)
                        multiply(gate_ps[v], x_hi[v], x_lo[v], 4 * n, n, m + GATES[n], n == 0, n == 3)
                    pe.wait_ge(h_ready, b + 1)
                    for n in range(4):
                        pe.wait_ge(y_read, 4 * b + n + 1)
                        multiply(down_ps[n % 2], h_hi, h_lo, 0, n, m + DOWNS[n], True, True)


def phase_combine(nc, io, keep):
    with ExitStack() as ctx:
        mem = Memory(nc, ctx)
        ye = [mem.sb(f"cb_y{s}", [P, D]) for s in range(2 * TT)]
        w_bc, sq = mem.sb("final_norm_rows", [P, D]), mem.sb("cb_square", [P, D])
        var, root, ms, rstd = (mem.sb("cb_" + n, [P, TT]) for n in ("var", "root", "ms", "rstd"))
        y_in = [mem.sem(f"cb_y_in{s}") for s in range(2 * TT)]
        w_in_, added, squared, ms_ready, root_done, dve_o, finished, stored = mem.sem(
            "cb_w_in", "cb_added", "cb_squared", "cb_ms_ready", "cb_root_done", "cb_dve_o", "cb_finished", "cb_stored")
        h = keep["h"]
        block = ctx.enter_context(nc.Block())

        @block.gpsimd
        def _(pool):
            for t in range(TT):
                for c in range(2):
                    n = 2 * t + c
                    pool.indirect_dma_start(ye[n][:], None, io["ys"],
                                            bass.IndirectOffsetOnAxis(ap=keep["slots"][:, c, t:t + 1], axis=0)
                                            ).then_inc(y_in[n], 16)

        @block.sync
        def _(sp):
            sp.dma_start(w_bc[:], io["final_norm_w"].rearrange("(a d) -> a d", a=1).to_broadcast([P, D])).then_inc(w_in_, 16)
            for t in range(TT):
                sp.wait_ge(finished, t + 1)
                sp.dma_start(io["out"][0, t * P:(t + 1) * P, :], h[:, t, :]).then_inc(stored, 16)
            sp.wait_ge(stored, 16 * TT)

        @block.scalar
        def _(act):
            for t in range(TT):
                act.wait_ge(added, 2 * t + 2)
                if t:
                    act.wait_ge(squared, t)
                act.activation(sq[:], h[:, t, :], ACT.Square, accum_out=var[:, t:t + 1]).then_inc(squared, 1)
                act.wait_ge(ms_ready, t + 1)
                act.activation(root[:, t:t + 1], ms[:, t:t + 1], ACT.Sqrt).then_inc(root_done, 1)

        @block.vector
        def _(dve):
            order = Order(dve, dve_o)

            def step(ins):
                order.done(ins)
                order.wait()

            def add(t):
                for c in range(2):
                    n = 2 * t + c
                    dve.wait_ge(y_in[n], 16)
                    if c:
                        dve.wait_ge(added, n)
                    dve.scalar_tensor_tensor(h[:, t, :], ye[n][:], keep["weights"][:, c, t:t + 1], h[:, t, :], ALU.mult,
                                             ALU.add).then_inc(added, 1)

            def norm(t):
                c = slice(t, t + 1)
                dve.wait_ge(squared, t + 1)
                dve.tensor_scalar(ms[:, c], var[:, c], 1.0 / D, NORM_EPS, ALU.mult, ALU.add).then_inc(ms_ready, 1)
                dve.wait_ge(root_done, t + 1)
                step(dve.reciprocal(rstd[:, c], root[:, c]))
                step(dve.tensor_tensor(var[:, c], rstd[:, c], rstd[:, c], ALU.mult))
                step(dve.tensor_tensor(var[:, c], var[:, c], ms[:, c], ALU.mult))
                step(dve.tensor_scalar(var[:, c], var[:, c], -0.5, 1.5, ALU.mult, ALU.add))
                step(dve.tensor_tensor(rstd[:, c], var[:, c], rstd[:, c], ALU.mult))
                dve.scalar_tensor_tensor(h[:, t, :], h[:, t, :], rstd[:, c], w_bc[:], ALU.mult, ALU.mult).then_inc(finished, 1)

            for t in range(TT):
                add(t)
                if t == 1:
                    dve.wait_ge(w_in_, 16)
                if t:
                    norm(t - 1)
            norm(TT - 1)


def build(nc, io):
    with ExitStack() as ctx:
        mem = Memory(nc, ctx)
        keep = {
            "const": mem.sb("const", [P, len(CONST), P]), "par": mem.sb("par", [P, P]), "one_ka": mem.sb("one_minus_k_a", [P, HEADS]),
            "lb": mem.sb("lb", [P, 4, HEADS]), "slots": mem.sb("slots", [P, 2, TT], U32), "weights": mem.sb("weights", [P, 2, TT]),
            "blk_expert": mem.sb("blk_expert", [1, MAX_BLOCKS + 2], I32), "n_blocks": mem.sb("n_blocks", [1, 1], I32),
            "pool_waits": mem.sem("pool_waits_passed"), "pe_waits": mem.sem("pe_waits_passed"),
        }
        with ExitStack() as inner:
            mem = Memory(nc, inner)
            keep["xn_hi"] = mem.sb("xn_hi", [P, KT, T], F32R)
            keep["xn_lo"] = mem.sb("xn_lo", [P, KT, T], F32R)
            phase_norm(nc, io, keep)
            phase_hgrn(nc, io, keep)
            phase_rwkv(nc, io, keep)
        mem = Memory(nc, ctx)
        keep["h_squares"] = mem.sb("h_squares", [P, TT, 4])
        keep["y_hi"], keep["h"] = mem.shared(("y_hi", [P, KT, T], F32R), ("h", [P, TT, D], F32))
        phase_merge(nc, io, keep)
        phase_route(nc, io, keep)
        phase_experts(nc, io, keep)
        phase_combine(nc, io, keep)


_INS = ["x", "norm_mix_w", "w_in", "hgrn_lb_raw", "hgrn_onorm_w", "rw_mu", "rw_w0", "rw_w_up", "rw_a0", "rw_a_up", "rw_g_up",
        "rw_k_k", "rw_k_a", "rw_r_k", "rw_ln_w", "rw_ln_b", "w_branch_hg", "w_branch_rw", "w_out", "norm_ffn_w",
        "router_group_w", "router_group_b", "router_expert_w", "router_expert_b", "expert_w_gate", "expert_w_up",
        "expert_w_down", "final_norm_w"]


def tensors(nc, arrays):
    io = {n: nc.dram_tensor(f"in_{n}_dram", a.shape, mybir.dt.from_np(a.dtype), kind="ExternalInput").ap()
          for n, a in arrays.items()}
    io["out"] = nc.dram_tensor("out_0_dram", (1, T, D), F32, kind="ExternalOutput").ap()
    for n, shape, dt in (("gate", (2 * KT, P, T), F32), ("y_hg", (HEADS, P, T), F32), ("y_rw", (HEADS, P, T), F32),
                         ("hn", (T, D), F32), ("slot_tok", (TABLE_BLOCKS * SLOTS, 1), U32),
                         ("ys", ((MAX_BLOCKS + 2) * SLOTS, D), F32)):
        io[n] = nc.dram_tensor(f"scratch_{n}", shape, dt).ap()
    return io


def kernel(**inputs):
    import concourse.bacc as _bacc
    from concourse.bass_utils import run_bass_kernel_spmd as _run

    nc = _bacc.Bacc("TRN2", target_bir_lowering=False, num_devices=1)
    arrays = {n: np.ascontiguousarray(inputs[n]) for n in _INS}
    arrays["square_constants"] = square_constants()
    build(nc, tensors(nc, arrays))
    r = _run(nc, [{f"in_{n}_dram": a for n, a in arrays.items()}], core_ids=[0])
    return r.results[0]["out_0_dram"]
```
